# Optimizing a Trainium2 kernel written in Bass

```python
import math
import jax, jax.numpy as jnp
from jax import lax
import numpy as np

D_MODEL = 1024
BATCH = 1
SEQ = 512
DEPTH = 2

N_A = DEPTH // 2
N_B = DEPTH - N_A
GDN_HEADS = 8
GDN_HEAD_DIM = D_MODEL // GDN_HEADS
GDN_CONV = 4
GDN_CHUNK = 64
SB_HEADS = 8
SB_HEAD_DIM = D_MODEL // SB_HEADS
SB_BLOCK = 128
D_FF = ((8 * D_MODEL // 3 + 127) // 128) * 128
FFN_CONV = 3
EPS = 1e-6

kernel_name = "yoco_gdn_stickbreaking_convffn"

def rmsnorm(x, g):
    xf = x.astype(jnp.float32)
    xf = xf * lax.rsqrt(jnp.mean(xf * xf, axis=-1, keepdims=True) + EPS)
    return (xf * g.astype(jnp.float32)).astype(x.dtype)

def l2norm(x):
    xf = x.astype(jnp.float32)
    return xf * lax.rsqrt(jnp.sum(xf * xf, axis=-1, keepdims=True) + EPS)

def causal_dwconv(x, w):
    K, C = w.shape
    return lax.conv_general_dilated(
        x, w[:, None, :].astype(x.dtype), window_strides=(1,), padding=[(K - 1, 0)],
        dimension_numbers=("NWC", "WIO", "NWC"), feature_group_count=C)

def gated_delta_rule(q, k, v, g, beta):
    B, T, H, Dk = q.shape
    Dv = v.shape[-1]
    C = GDN_CHUNK
    N = T // C
    f32 = jnp.float32

    def chunks(t):
        t = t.astype(f32).reshape((B, N, C, H) + t.shape[3:])
        return jnp.moveaxis(t, 3, 1)

    q, k, v, beta = chunks(q), chunks(k), chunks(v), chunks(beta)
    g = jnp.cumsum(chunks(g), axis=-1)
    tri = jnp.tril(jnp.ones((C, C), dtype=bool))
    strict = jnp.tril(jnp.ones((C, C), dtype=bool), -1)
    decay = jnp.exp(jnp.where(tri, g[..., :, None] - g[..., None, :], -jnp.inf))
    k_beta = k * beta[..., None]
    L = jnp.where(strict, jnp.einsum("bhnid,bhnjd->bhnij", k_beta, k) * decay, 0.0)
    rhs = jnp.concatenate([v * beta[..., None], k_beta * jnp.exp(g)[..., None]], axis=-1)
    sol = lax.linalg.triangular_solve(L, rhs, left_side=True, lower=True, unit_diagonal=True)
    u, w = sol[..., :Dv], sol[..., Dv:]
    qk = jnp.where(tri, jnp.einsum("bhnid,bhnjd->bhnij", q, k) * decay, 0.0)
    g_last = g[..., -1]
    q_dec = q * jnp.exp(g)[..., None]
    k_dec = k * jnp.exp(g_last[..., None] - g)[..., None]

    def step(S, inp):
        qk_i, q_dec_i, k_dec_i, u_i, w_i, gl_i = inp
        v_new = u_i - jnp.einsum("bhck,bhkv->bhcv", w_i, S)
        o = jnp.einsum("bhck,bhkv->bhcv", q_dec_i, S) + jnp.einsum("bhij,bhjv->bhiv", qk_i, v_new)
        S = S * jnp.exp(gl_i)[..., None, None] + jnp.einsum("bhck,bhcv->bhkv", k_dec_i, v_new)
        return S, o

    xs = tuple(jnp.moveaxis(t, 2, 0) for t in (qk, q_dec, k_dec, u, w, g_last))
    S0 = jnp.zeros((B, H, Dk, Dv), f32)
    _, o = lax.scan(step, S0, xs)
    return jnp.transpose(o, (1, 0, 3, 2, 4)).reshape(B, T, H, Dv)

def gdn_mixer(h, w_in, conv_w, a_log, dt_bias, o_gain, w_out):
    B, T, D = h.shape
    H, Dh = GDN_HEADS, GDN_HEAD_DIM
    proj = h @ w_in
    qkv, z, a, b = jnp.split(proj, [3 * D, 4 * D, 4 * D + H], axis=-1)
    qkv = jax.nn.silu(causal_dwconv(qkv, conv_w))
    q, k, v = jnp.split(qkv, 3, axis=-1)
    q = l2norm(q.reshape(B, T, H, Dh)) * (Dh ** -0.5)
    k = l2norm(k.reshape(B, T, H, Dh))
    v = v.reshape(B, T, H, Dh)
    g = -jnp.exp(a_log.astype(jnp.float32)) * jax.nn.softplus(
        a.astype(jnp.float32) + dt_bias.astype(jnp.float32))
    beta = jax.nn.sigmoid(b.astype(jnp.float32))
    o = gated_delta_rule(q, k, v, g, beta)
    o = rmsnorm(o, o_gain) * jax.nn.silu(z.reshape(B, T, H, Dh).astype(jnp.float32))
    return o.reshape(B, T, D).astype(h.dtype) @ w_out

def stick_breaking_attention(q, k, v):
    B, H, T, D = q.shape
    scale = D ** -0.5
    outs = []
    for blk in range(T // SB_BLOCK):
        lo, hi = blk * SB_BLOCK, (blk + 1) * SB_BLOCK
        z = jnp.einsum("bhtd,bhsd->bhts", q[:, :, lo:hi], k[:, :, :hi],
                       preferred_element_type=jnp.float32) * scale
        t_idx = lo + jnp.arange(SB_BLOCK)[:, None]
        s_idx = jnp.arange(hi)[None, :]
        causal = s_idx < t_idx
        log_fail = jnp.where(causal, jax.nn.log_sigmoid(-z), 0.0)
        after = lax.cumsum(log_fail, axis=3, reverse=True) - log_fail
        a = jnp.where(causal, jnp.exp(jax.nn.log_sigmoid(z) + after), 0.0)
        outs.append(jnp.einsum("bhts,bhsd->bhtd", a, v[:, :, :hi].astype(jnp.float32)))
    return jnp.concatenate(outs, axis=2).astype(q.dtype)

def conv_ffn(h, w_up, conv_w, w_down):
    u = causal_dwconv(h @ w_up, conv_w)
    gate, up = jnp.split(u, 2, axis=-1)
    return (jax.nn.silu(gate) * up) @ w_down

def setup_inputs(seed: int = 0) -> dict:
    key = jax.random.key(seed)
    ks = jax.random.split(key, 20)
    D, H = D_MODEL, GDN_HEADS
    f32 = jnp.float32
    out_scale = (2 * DEPTH) ** -0.5

    def nrm(k, shape, fan_in, gain=1.0):
        return jax.random.normal(k, shape, f32) * (gain * fan_in ** -0.5)

    def gvec(k, shape):
        return 1.0 + 0.02 * jax.random.normal(k, shape, f32)

    dt = jnp.exp(jax.random.uniform(ks[4], (N_A, H), f32, math.log(1e-3), math.log(1e-1)))
    return {
        "x": jax.random.normal(ks[0], (BATCH, SEQ, D), f32),
        "a_norm": gvec(ks[1], (N_A, D)),
        "a_w_in": nrm(ks[2], (N_A, D, 4 * D + 2 * H), D),
        "a_conv": nrm(ks[3], (N_A, GDN_CONV, 3 * D), GDN_CONV),
        "a_log": jnp.log(jax.random.uniform(ks[5], (N_A, H), f32, 1.0, 16.0)),
        "a_dt_bias": dt + jnp.log(-jnp.expm1(-dt)),
        "a_out_norm": gvec(ks[6], (N_A, GDN_HEAD_DIM)),
        "a_w_out": nrm(ks[7], (N_A, D, D), D, out_scale),
        "kv_norm": gvec(ks[8], (D,)),
        "w_kv": nrm(ks[9], (D, 2 * D), D),
        "k_norm": gvec(ks[10], (SB_HEAD_DIM,)),
        "b_norm": gvec(ks[11], (N_B, D)),
        "b_w_q": nrm(ks[12], (N_B, D, D), D),
        "q_norm": gvec(ks[13], (N_B, SB_HEAD_DIM)),
        "b_w_out": nrm(ks[14], (N_B, D, D), D, out_scale),
        "ffn_norm": gvec(ks[15], (DEPTH, D)),
        "ffn_w_up": nrm(ks[16], (DEPTH, D, 2 * D_FF), D),
        "ffn_conv": nrm(ks[17], (DEPTH, FFN_CONV, 2 * D_FF), FFN_CONV),
        "ffn_w_down": nrm(ks[18], (DEPTH, D_FF, D), D_FF, out_scale),
    }

def reference(x, a_norm, a_w_in, a_conv, a_log, a_dt_bias, a_out_norm, a_w_out,
              kv_norm, w_kv, k_norm, b_norm, b_w_q, q_norm, b_w_out,
              ffn_norm, ffn_w_up, ffn_conv, ffn_w_down):
    B, T, D = x.shape
    H, Dh = SB_HEADS, SB_HEAD_DIM
    for layer in range(DEPTH):
        if layer < N_A:
            x = x + gdn_mixer(rmsnorm(x, a_norm[layer]), a_w_in[layer], a_conv[layer],
                              a_log[layer], a_dt_bias[layer], a_out_norm[layer], a_w_out[layer])
        else:
            j = layer - N_A
            if j == 0:
                kv = rmsnorm(x, kv_norm) @ w_kv
                k_s, v_s = jnp.split(kv, 2, axis=-1)
                k_s = jnp.transpose(rmsnorm(k_s.reshape(B, T, H, Dh), k_norm), (0, 2, 1, 3))
                v_s = jnp.transpose(v_s.reshape(B, T, H, Dh), (0, 2, 1, 3))
            q = rmsnorm((rmsnorm(x, b_norm[j]) @ b_w_q[j]).reshape(B, T, H, Dh), q_norm[j])
            o = stick_breaking_attention(jnp.transpose(q, (0, 2, 1, 3)), k_s, v_s)
            x = x + jnp.transpose(o, (0, 2, 1, 3)).reshape(B, T, D) @ b_w_out[j]
        x = x + conv_ffn(rmsnorm(x, ffn_norm[layer]), ffn_w_up[layer], ffn_conv[layer], ffn_w_down[layer])
    return x


_drawn_inputs = setup_inputs


def setup_inputs(seed=0):
    import zlib

    import numpy as np

    out = dict(_drawn_inputs(seed))
    spreads = {}
    factors = {'a_norm': 5.061,
     'a_out_norm': 8.0,
     'kv_norm': 21.665,
     'k_norm': 8.0,
     'b_norm': 21.947,
     'q_norm': 23.018,
     'ffn_norm': 4.849}
    for name, (base, spread) in spreads.items():
        noise = np.random.default_rng([zlib.crc32(name.encode()), seed]).standard_normal(out[name].shape)
        drawn = base * np.exp(spread * noise) if base else spread * noise
        out[name] = __import__('jax').numpy.asarray(drawn.astype(out[name].dtype))
    for name, factor in factors.items():
        out[name] = (out[name] * factor).astype(out[name].dtype)
    return out
```

```python
from contextlib import ExitStack

import numpy as np

import concourse.bass as bass
from concourse import mybir

ALU = mybir.AluOpType
ACT = mybir.ActivationFunctionType
F32 = mybir.dt.float32
F32R = mybir.dt.float32r

P = 128
D = 1024
T = 512
KT = D // P
NB = T // P
H = 8
DFF = 2816
FT = DFF // P
EPS = 1e-6
NEG = -1e30
LEVELS = 7
LN_EXP = "natural_log_exp_and_others"
AHEAD = 3

U_GDN = 0
U_GDN_OUT = U_GDN + 4 * H
U_UP = [U_GDN_OUT + KT, 0]
U_DOWN = [U_UP[0] + 2 * FT, 0]
U_ATT = U_DOWN[0] + 3 * KT
U_ATT_OUT = U_ATT + 3 * H
U_UP[1] = U_ATT_OUT + KT
U_DOWN[1] = U_UP[1] + 2 * FT
UNITS = U_DOWN[1] + 3 * KT
DOWN_KT = [8, 8, FT - 16]

G_NORM = {"a": 0, "ffn0": 8, "kv": 16, "b": 24, "ffn1": 32}
C_GDN_CONV = 40
C_FFN_CONV = C_GDN_CONV + H * 12
C_OGAIN = C_FFN_CONV + 2 * FT * 6
C_KGAIN = C_OGAIN + 1
C_QGAIN = C_KGAIN + 1
C_ALOG = C_QGAIN + 1
C_DT = C_ALOG + 1
PARAMS = C_DT + 1


def trunk(nc, x, weights, w_ab, params, masks, out, g_rows):
    with ExitStack() as ctx:
        sb = lambda n, s, d=F32: ctx.enter_context(nc.sbuf_tensor(n, s, d))

        xs = sb("x_stream", [P, KT, T])
        h_hi, h_lo = sb("h_hi", [P, KT, T], F32R), sb("h_lo", [P, KT, T], F32R)
        raw = sb("w_raw", [P, 4, 8 * P])
        w_hi, w_lo = sb("w_hi", [P, 4, 8 * P], F32R), sb("w_lo", [P, 4, 8 * P], F32R)
        prm = sb("params", [P, PARAMS])
        ones = sb("ones", [P, P])
        rms = sb("rms", [P, T])
        hg = sb("h_scaled", [P, T])
        sumsq = sb("sumsq", [P, T])
        ms, nt = sb("mean_sq", [P, T]), sb("newton_t", [P, T])
        taps = sb("taps", [P, 12])
        gains = sb("gains_now", [P, 4])

        with ExitStack() as a:
            sa = lambda n, s, d=F32: a.enter_context(nc.sbuf_tensor(n, s, d))
            lvl = sa("level_masks", [P, LEVELS, P])
            ident = sa("ident", [P, P])
            tri = sa("tri_neg", [P, P])
            o_hi, o_lo = sa("o_hi", [P, H, T], F32R), sa("o_lo", [P, H, T], F32R)
            gspread = sa("g_spread", [P, T])
            decay = sa("decay", [P, T])
            egb = sa("exp_g", [P, T])
            gcols = sa("g_cols", [P, H, 12])
            cols = sa("cols_now", [P, 16])
            cin = sa("conv_in", [P, 3 + T])
            kqv = sa("kqv", [P, 3, T])
            zraw, zs = sa("z_raw", [P, T]), sa("z_silu", [P, T])
            r_kq = sa("r_kq", [P, 3, T])
            m_kq = sa("m_kq", [P, 3, T])
            osb, tz = sa("o_raw", [P, T]), sa("o_gated", [P, T])
            vn = sa("v_new", [P, T])
            st = sa("state", [P, P])
            with ExitStack() as b:
                sab = lambda n, s, d=F32: b.enter_context(nc.sbuf_tensor(n, s, d))
                ab = sab("ab_rows", [40, T])
                gb = sab("g_beta_rows", [40, T])
                row1, row2, row3 = (sab(f"row{i}", [H, T]) for i in range(3))
                onesrow = sab("ones_rows", [H, T])
                aexp = sab("a_exp", [H, 1])
                wab_hi, wab_lo = sab("wab_hi", [P, 8 * P], F32R), sab("wab_lo", [P, 8 * P], F32R)
            ktok, vtok, kdec = sa("k_tok", [P, T]), sa("v_tok", [P, T]), sa("k_dec", [P, T])
            lt, qkt, qe = sa("lt", [P, T]), sa("qk_t", [P, T]), sa("q_exp", [P, T])
            ct = sa("c_levels", [P, 3, T])
            xm, xt = sa("inv", [P, T]), sa("inv_t", [P, T])
            m1 = sa("m1", [P, T])
            xte, nwt = xm, m1
        kn, qn = kqv[:, 0, :], kqv[:, 1, :]
        n_k, n_o = hg, nt
        h_scaled = (hg, vn)
        x_sq = (zraw, zs, osb, tz)
        with ExitStack() as a:
            sa = lambda n, s, d=F32: a.enter_context(nc.sbuf_tensor(n, s, d))
            hid_hi, hid_lo = sa("hid_hi", [P, FT, T], F32R), sa("hid_lo", [P, FT, T], F32R)
            fin = sa("ffn_conv_in", [P, 2, 2 + T])
            facc = sa("ffn_conv_acc", [P, 2, T])
            fh = facc[:, 1, :]
        SW = sum(P * (b + 1) for b in range(NB))
        with ExitStack() as a:
            sa = lambda n, s, d=F32: a.enter_context(nc.sbuf_tensor(n, s, d))
            ao_hi, ao_lo = sa("att_o_hi", [P, H, T], F32R), sa("att_o_lo", [P, H, T], F32R)
            hb_hi, hb_lo = sa("hb_hi", [P, KT, T], F32R), sa("hb_lo", [P, KT, T], F32R)
            aident, amask = sa("att_ident", [P, P]), sa("att_mask", [P, P])
            araw = sa("kqv_att", [P, 3, T])
            am, ar = sa("kq_ams", [P, 2, T]), sa("kq_ar", [P, 2, T])
            avtok = sa("att_v_tok", [P, T])
            sfail, shit = sa("fail", [P, SW]), sa("hit", [P, SW])
            surv = sa("survive", [P, SW + NB])
        akt, aqt = araw[:, 0, :], araw[:, 1, :]
        aw = shit
        awt = sfail
        OFF = [sum(P * (b + 1) for b in range(n)) for n in range(NB)]

        ps = ctx.enter_context(nc.psum_tensor("ps", [P, 8, T], F32))
        B_SUM, B_M, B_P, B_Q, B_T, B_O = 2, 3, 4, 5, 6, 7
        F_BANK = (0, 1, B_M, B_P)
        A_BANK = (0, 1, B_T)
        A_PASSES = (0, 4, 8, 12, 16, 20, 24, 29, 34, 39, 44, 48, 51, 55, 58, 62, 65, 69, 72)
        A_ENDS = (5, 10, 17)

        def sem(name):
            return ctx.enter_context(nc.semaphore(name))

        s_w_loaded = [sem(f"w_loaded_{i}") for i in range(4)]
        s_att_w_loaded = [sem(f"att_w_loaded_{i}") for i in range(3)]
        s_x_loaded = [sem(f"x_loaded_{k}") for k in range(KT)]
        s_a_exp_done = sem("a_exp_done")
        s_ab_summed = sem("ab_summed")
        s_ab_taken = sem("ab_taken")
        s_ak_normed = sem("ak_normed")
        s_akq_guess = sem("akq_guess")
        s_akq_ln = sem("akq_ln")
        s_akq_ms_taken = sem("akq_ms_taken")
        s_akq_newton = sem("akq_newton")
        s_akq_rnorm = sem("akq_rnorm")
        s_akq_squared = sem("akq_squared")
        s_akq_summed = sem("akq_summed")
        s_ao_done = sem("ao_done")
        s_ao_hi_done = sem("ao_hi_done")
        s_ao_lo_done = sem("ao_lo_done")
        s_aones_set = sem("aones_set")
        s_aq_normed = sem("aq_normed")
        s_att_evacuated = sem("att_evacuated")
        s_att_masks_loaded = sem("att_masks_loaded")
        s_av_tok_done = sem("av_tok_done")
        s_av_turned = sem("av_turned")
        s_aw_done = sem("aw_done")
        s_aw_turned = sem("aw_turned")
        s_awt_taken = sem("awt_taken")
        s_beta_done = sem("beta_done")
        s_c0_done = sem("c0_done")
        s_c0_turned = sem("c0_turned")
        s_c_done = sem("c_done")
        s_cols_now = sem("cols_now")
        s_conv_done = sem("conv_done")
        s_conv_pads = sem("conv_pads")
        s_decay_arg = sem("decay_arg")
        s_decay_done = sem("decay_done")
        s_e_done = sem("e_done")
        s_exp_g_cols = sem("exp_g_cols")
        s_exp_g_done = sem("exp_g_done")
        s_ffn_conv_done = sem("ffn_conv_done")
        s_ffn_evacuated = sem("ffn_evacuated")
        s_ffn_pads = sem("ffn_pads")
        s_ffn_taps = sem("ffn_taps")
        s_g_cols_done = sem("g_cols_done")
        s_g_cols_in = sem("g_cols_in")
        s_g_diff = sem("g_diff")
        s_g_scanned = sem("g_scanned")
        s_g_spread = sem("g_spread")
        s_g_stored = sem("g_stored")
        s_gate_silu = sem("gate_silu")
        s_gb_cleared = sem("gb_cleared")
        s_gb_turned = sem("gb_turned")
        s_gdn_evacuated = sem("gdn_evacuated")
        s_h_hi_done = sem("h_hi_done")
        s_h_lo_done = sem("h_lo_done")
        s_h_scaled_done = sem("h_scaled_done")
        s_hb_hi_done = sem("hb_hi_done")
        s_hb_lo_done = sem("hb_lo_done")
        s_hb_scaled_done = sem("hb_scaled_done")
        s_hid_hi_done = sem("hid_hi_done")
        s_hid_lo_done = sem("hid_lo_done")
        s_hidden_done = sem("hidden_done")
        s_inv_done = sem("inv_done")
        s_inv_t0_done = sem("inv_t0_done")
        s_inv_t_done = sem("inv_t_done")
        s_inv_te_done = sem("inv_te_done")
        s_k_dec_done = sem("k_dec_done")
        s_k_normed = sem("k_normed")
        s_k_tok_done = sem("k_tok_done")
        s_k_turned = sem("k_turned")
        s_kk_done = sem("kk_done")
        s_kn_steps = sem("kn_steps")
        s_kq_done = sem("kq_done")
        s_kq_guess = sem("kq_guess")
        s_kq_ln = sem("kq_ln")
        s_kq_rnorm = sem("kq_rnorm")
        s_kq_silu = sem("kq_silu")
        s_kq_squared = sem("kq_squared")
        s_kq_summed = sem("kq_summed")
        s_level_done = sem("level_done")
        s_ln_done = sem("ln_done")
        s_lt_done = sem("lt_done")
        s_m1_done = sem("m1_done")
        s_m1_taken = sem("m1_taken")
        s_masks_loaded = sem("masks_loaded")
        s_ms_taken_kq = sem("ms_taken_kq")
        s_ms_taken_o = sem("ms_taken_o")
        s_neg_abs_done = sem("neg_abs_done")
        s_nwt_done = sem("nwt_done")
        s_nwt_taken = sem("nwt_taken")
        s_o_correction = sem("o_correction")
        s_o_done = sem("o_done")
        s_o_gated = sem("o_gated")
        s_o_guess = sem("o_guess")
        s_o_hi_done = sem("o_hi_done")
        s_o_ln = sem("o_ln")
        s_o_lo_done = sem("o_lo_done")
        s_o_newton = sem("o_newton")
        s_o_out = sem("o_out")
        s_o_squared = sem("o_squared")
        s_o_summed = sem("o_summed")
        s_o_taken = sem("o_taken")
        s_one_plus_e = sem("one_plus_e")
        s_ones_rows_set = sem("ones_rows_set")
        s_ones_set = sem("ones_set")
        s_out_stored = sem("out_stored")
        s_params_loaded = sem("params_loaded")
        s_q_exp_done = sem("q_exp_done")
        s_q_normed = sem("q_normed")
        s_qkt_done = sem("qkt_done")
        s_rms_done = sem("rms_done")
        s_rms_newton = sem("rms_newton")
        s_row_step = sem("row_step")
        s_scan_done = sem("scan_done")
        s_scores_done = sem("scores_done")
        s_scores_masked = sem("scores_masked")
        s_sig_done = sem("sig_done")
        s_sq_done = sem("sq_done")
        s_state_done = sem("state_done")
        s_state_summed = sem("state_summed")
        s_stream_added = sem("stream_added")
        s_stream_guess = sem("stream_guess")
        s_stream_ln = sem("stream_ln")
        s_stream_ms_done = sem("stream_ms_done")
        s_stream_summed = sem("stream_summed")
        s_sumsq_done = sem("sumsq_done")
        s_taps_now = sem("taps_now")
        s_unit_used = sem("unit_used")
        s_v_new_done = sem("v_new_done")
        s_v_scaled = sem("v_scaled")
        s_v_silu = sem("v_silu")
        s_v_tok_done = sem("v_tok_done")
        s_v_turned = sem("v_turned")
        s_w_hi_done = sem("w_hi_done")
        s_w_lo_done = sem("w_lo_done")
        s_wab_hi_done = sem("wab_hi_done")
        s_wab_loaded = sem("wab_loaded")
        s_wab_split = sem("wab_split")
        s_x_final = sem("x_final")
        s_x_squared = sem("x_squared")
        s_z_silu = sem("z_silu")

        def due(n):
            return not (isinstance(n, int) and n <= 0)

        def blocks(ap):
            return ap.rearrange("p (c i) -> p c i", c=NB)

        def per_block(col):
            return col.unsqueeze(2).to_broadcast([P, NB, P])

        def each_block(ap):
            return ap.unsqueeze(1).to_broadcast([P, NB, P])

        def half(ap, k, bit):
            return ap.rearrange("p (g t w) -> p g t w", t=2, w=1 << k)[:, :, bit, :]

        def whole(ap, k):
            return ap.rearrange("p (g w) -> p g w", w=1 << k)

        def lap_of(u):
            return u // 4 - (3 * H // 4 if u >= U_ATT_OUT else 0)

        blk = ctx.enter_context(nc.Block())

        @blk.sync
        def _(sp):
            def load(u, slot, cols_=8 * P, loaded=s_w_loaded):
                if due(u - AHEAD + 1):
                    sp.wait_ge(s_w_hi_done, u - AHEAD + 1)
                if due(u - AHEAD + 1):
                    sp.wait_ge(s_w_lo_done, u - AHEAD + 1)
                sp.dma_start(raw[:, slot, 0:cols_], weights[u, :, 0:cols_]).then_inc(loaded[slot], 16)

            sp.dma_start(prm[:], params).then_inc(s_params_loaded, 16)
            for k in range(KT):
                sp.dma_start(xs[:, k, :], x[k]).then_inc(s_x_loaded[k], 16)
                if k == 1:
                    sp.dma_start(raw[:, 3, :], w_ab).then_inc(s_wab_loaded, 16)
                    load(0, 0)
            load(1, 1)
            load(2, 2)
            for dst, m in ((lvl[:].rearrange("p l i -> p (l i)"), masks[:, 0:LEVELS * P]),
                           (ident[:], masks[:, LEVELS * P:(LEVELS + 1) * P]),
                           (tri[:], masks[:, (LEVELS + 1) * P:(LEVELS + 2) * P])):
                sp.dma_start(dst, m).then_inc(s_masks_loaded, 16)
            sp.wait_ge(s_wab_split, 2)
            load(3, 3)
            load(4, 0)
            load(5, 1)
            sp.wait_ge(s_g_scanned, NB)
            sp.dma_start(g_rows, gb[0:H, :]).then_inc(s_g_stored, 16)
            sp.wait_ge(s_g_stored, 16)

            def spread_g(h):
                if due(h):
                    sp.wait_ge(s_g_diff, h)
                if due(h):
                    sp.wait_ge(s_exp_g_done, h)
                sp.dma_start(gspread[:], g_rows[h].partition_broadcast(P)).then_inc(s_g_spread, 16)

            spread_g(0)
            load(6, 2)
            load(7, 3)
            spread_g(1)
            with sp.Fori(2, H) as i:
                for s in range(4):
                    load(i * 4 + s, s)
                spread_g(i)
            with sp.Fori(H, (U_UP[0] - U_GDN) // 4) as i:
                for s in range(4):
                    load(i * 4 + s, s)
            for layer in range(2):
                with sp.Fori(0, 2 * FT // 4) as i:
                    for s in range(4):
                        load(U_UP[layer] + i * 4 + s, s)
                with sp.Fori(0, 2) as i:
                    for n in range(12):
                        load(U_DOWN[layer] + i * 12 + n, n % 4, DOWN_KT[n % 3] * P)
                if layer == 0:
                    with sp.Fori(0, H) as i:
                        for s in range(3):
                            load(U_ATT + i * 3 + s, s, loaded=s_att_w_loaded)
                    with sp.Fori(0, KT // 4) as i:
                        for s in range(4):
                            load(U_ATT_OUT + i * 4 + s, s)
            for m in range(KT):
                sp.wait_ge(s_x_final, m + 1)
                sp.dma_start(out[m], xs[:, m, :]).then_inc(s_out_stored, 16)
            sp.wait_ge(s_out_stored, 16 * KT)

        @blk.tensor
        def _(pe):
            def three(acc, slot, k, r_hi, r_lo, first, last, passes=(0, 1, 2)):
                mm = None
                for p in passes:
                    w, r = ((w_hi, r_hi), (w_lo, r_hi), (w_hi, r_lo))[p]
                    mm = pe.matmul(acc, w[:, slot, k * P:(k + 1) * P], r,
                                   start=first and p == 0, stop=last and p == 2)
                return mm

            def unit_ready(u):
                pe.wait_ge(s_w_hi_done, u + 1)
                pe.wait_ge(s_w_lo_done, u + 1)

            def sum_partitions(bank, src):
                return pe.matmul(ps[:, bank, :], ones[:], src, start=True, stop=True)

            def stream_sum(n):
                if due(n * KT):
                    pe.wait_ge(s_sumsq_done, n * KT)
                sum_partitions(B_SUM, sumsq[:]).then_inc(s_stream_summed, 1)

            pe.wait_ge(s_ones_set, 1)
            pe.wait_ge(s_wab_split, 2)
            unit_ready(0)
            for k in range(KT):
                pe.wait_ge(s_h_hi_done, k + 1)
                pe.wait_ge(s_h_lo_done, k + 1)
                for w, r in ((wab_hi, h_hi), (wab_lo, h_hi), (wab_hi, h_lo)):
                    mm = pe.matmul(ps[:, B_M, :], w[:, k * P:(k + 1) * P], r[:, k, :],
                                   start=(k == 0 and w is wab_hi and r is h_hi),
                                   stop=(k == KT - 1 and r is h_lo))
                if k == KT - 1:
                    mm.then_inc(s_ab_summed, 1)
                mm = three(ps[:, 0, :], 0, k, h_hi[:, k, :], h_lo[:, k, :], k == 0, k == KT - 1)
            mm.then_inc(s_unit_used, 1)
            stream_sum(1)

            def project(hn, s):
                for n in range(4 * s, 4 * s + 4):
                    j, k, p = n // 24, n % 24 // 3, n % 3
                    if n % 24 == 0:
                        unit_ready(hn * 4 + j)
                        if due(hn * 4 + j - 1):
                            pe.wait_ge(s_gdn_evacuated, hn * 4 + j - 1)
                    mm = three(ps[:, j % 2, :], j, k, h_hi[:, k, :], h_lo[:, k, :], k == 0, k == KT - 1, (p,))
                    if n % 24 == 23:
                        mm.then_inc(s_unit_used, 1)

            def out_early(base, n, r_hi, r_lo, kts):
                m, kt, p = n // (3 * kts), n % (3 * kts) // 3, n % 3
                if n % (3 * kts) == 0:
                    unit_ready(base + m)
                three(ps[:, F_BANK[m], :], m, kt, r_hi[:, kt, :], r_lo[:, kt, :], kt == 0, False, (p,))

            def norm_sums(hn, s, first=False):
                if s in (14 if first else 12, 18):
                    j = s // 18
                    if due(hn * 2 + j + 1):
                        pe.wait_ge(s_kq_squared, hn * 2 + j + 1)
                    if due(hn - 1):
                        pe.wait_ge(s_ms_taken_o, hn - 1)
                    if due(hn * 2 + j):
                        pe.wait_ge(s_ms_taken_kq, hn * 2 + j)
                    sum_partitions(B_SUM, r_kq[:, j, :]).then_inc(s_kq_summed, 1)

            def o_sum(h, kq_sums):
                pe.wait_ge(s_o_squared, h + 1)
                if due(kq_sums):
                    pe.wait_ge(s_ms_taken_kq, kq_sums)
                if due(h):
                    pe.wait_ge(s_ms_taken_o, h)
                sum_partitions(B_SUM, r_kq[:, 2, :]).then_inc(s_o_summed, 1)

            def each(fn, bank):
                for c in range(NB):
                    cs = slice(c * P, (c + 1) * P)
                    mm = fn(ps[:, bank, cs], cs)
                return mm

            def delta(h, s):
                if s == 0:
                    pe.wait_ge(s_k_normed, h + 1)
                    if due(4 * h):
                        pe.wait_ge(s_v_scaled, 4 * h)
                    if due(3 * h):
                        pe.wait_ge(s_state_done, 3 * h)
                    each(lambda o, c: pe.transpose(o, kqv[:, 0, c], ident[:]), B_T).then_inc(s_k_turned, 1)
                    each(lambda o, c: pe.matmul(o, kqv[:, 0, c], kqv[:, 0, c], start=True, stop=True), B_M)\
                        .then_inc(s_kk_done, 1)
                if s == 1:
                    pe.wait_ge(s_q_normed, h + 1)
                    if due(h):
                        pe.wait_ge(s_nwt_taken, h)
                    if due(6 * h):
                        pe.wait_ge(s_inv_t_done, 6 * h)
                    pe.wait_ge(s_v_silu, h + 1)
                    each(lambda o, c: pe.matmul(o, kqv[:, 0, c], kqv[:, 1, c], start=True, stop=True), B_P)\
                        .then_inc(s_kq_done, 1)
                    each(lambda o, c: pe.transpose(o, kqv[:, 2, c], ident[:]), B_Q).then_inc(s_v_turned, 1)
                if s == 2:
                    pe.wait_ge(s_c0_done, h + 1)
                    pe.wait_ge(s_lt_done, 2 * h + 1)
                    each(lambda o, c: pe.matmul(o, ct[:, 0, c], ident[:], start=True, stop=True), B_M)\
                        .then_inc(s_c0_turned, 1)
                if s in (3, 5, 7, 9, 11, 13):
                    k = (s - 1) // 2
                    if due(6 * h + k):
                        pe.wait_ge(s_c_done, 6 * h + k)
                    if due(6 * h + k):
                        pe.wait_ge(s_inv_done, 6 * h + k)
                    if k > 1:
                        if due(6 * h + k - 1):
                            pe.wait_ge(s_m1_taken, 6 * h + k - 1)
                    each(lambda o, c: pe.matmul(o, ct[:, k % 3, c], xm[:, c], start=True, stop=True), B_M)\
                        .then_inc(s_m1_done, 1)
                if s in (4, 6, 8, 10, 12, 14):
                    k = (s - 2) // 2
                    if due(6 * h + k):
                        pe.wait_ge(s_m1_taken, 6 * h + k)
                    if k == 1:
                        pe.wait_ge(s_inv_t0_done, h + 1)
                        pe.wait_ge(s_qkt_done, h + 1)
                        pe.wait_ge(s_v_tok_done, h + 1)
                    if due(6 * h + k - 1):
                        pe.wait_ge(s_inv_t_done, 6 * h + k - 1)
                    for c in range(NB):
                        cs, at = slice(c * P, (c + 1) * P), slice(c * P // 2, (c + 1) * P // 2)
                        if k < 6:
                            pe.matmul(whole(ps[:, B_P, at], k), xt[:, cs], half(m1[:, cs], k, 0),
                                      start=True, stop=True)
                        mm = pe.matmul(whole(ps[:, B_Q, at], k), m1[:, cs], half(xt[:, cs], k, 1),
                                       start=True, stop=True)
                    mm.then_inc(s_level_done, 1)
                if s == 15:
                    pe.wait_ge(s_inv_te_done, h + 1)
                    pe.wait_ge(s_inv_done, 6 * h + 6)
                    pe.wait_ge(s_k_tok_done, h + 1)
                    each(lambda o, c: pe.matmul(o, ktok[:, c], xte[:, c], start=True, stop=True), B_P)\
                        .then_inc(s_nwt_done, 1)
                if s >= 16:
                    c = (s - 16) // 2
                    cs = slice(c * P, (c + 1) * P)
                    if s % 2 == 0:
                        if c == 0:
                            pe.wait_ge(s_k_dec_done, h + 1)
                            pe.wait_ge(s_k_tok_done, h + 1)
                        if due(3 * h + c):
                            pe.wait_ge(s_state_done, 3 * h + c)
                        mm = pe.matmul(ps[:, B_T, cs], xt[:, cs], vtok[:, cs], start=True, stop=c == 0)
                        if c:
                            pe.wait_ge(s_nwt_taken, h + 1)
                            mm = pe.matmul(ps[:, B_T, cs], nwt[:, cs], st[:], start=False, stop=True)
                        mm.then_inc(s_v_new_done, 1)
                    else:
                        if c == 0:
                            if due(h):
                                pe.wait_ge(s_o_taken, h)
                            pe.wait_ge(s_m1_taken, 6 * h + 6)
                        if c:
                            pe.wait_ge(s_q_exp_done, h + 1)
                            pe.matmul(ps[:, B_O, cs], st[:], qe[:, cs], start=True, stop=False)
                        pe.wait_ge(s_v_scaled, 4 * h + c + 1)
                        mm = pe.matmul(ps[:, B_O, cs], vn[:, cs], qkt[:, cs], start=c == 0, stop=True)
                        if c < NB - 1:
                            mm = pe.matmul(ps[:, B_M, 0:P], kdec[:, cs], vn[:, cs], start=True, stop=True)
                            mm.then_inc(s_state_summed, 1)
                        else:
                            mm.then_inc(s_o_done, 1)

            for s in range(6, 24):
                project(0, s)
                norm_sums(0, s, first=True)
                if s == 14:
                    pe.wait_ge(s_g_scanned, NB)
                    pe.wait_ge(s_beta_done, 1)
                    pe.wait_ge(s_masks_loaded, 16 * 3)
                    for c in range(NB):
                        mm = pe.transpose(ps[:, B_T, c * 40:(c + 1) * 40], gb[:, c * P:(c + 1) * P],
                                          ident[0:40, 0:40])
                    mm.then_inc(s_gb_turned, 1)
            def gdn_tile(k):
                pe.wait_ge(s_o_lo_done, k + 1)
                pe.wait_ge(s_o_hi_done, k + 1)

            def gdn_head(h, prev, more):
                for s in range(24):
                    if more and s in (3, 15):
                        project(h + 1, s)
                    delta(h, s)
                    if prev and s == 3:
                        o_sum(h - 1, 2 * h + 2)
                    if more:
                        if s not in (3, 15):
                            project(h + 1, s)
                        norm_sums(h + 1, s)
                    elif s < 18:
                        if s == 0:
                            pe.wait_ge(s_gdn_evacuated, 4 * H)
                            pe.wait_ge(s_o_hi_done, H - 2)
                            pe.wait_ge(s_o_lo_done, H - 2)
                        for n in (2 * s, 2 * s + 1):
                            out_early(U_GDN_OUT, n, o_hi, o_lo, H - 2)

            gdn_head(0, False, True)
            gdn_head(1, True, True)
            with pe.Fori(2, H - 1) as h:
                gdn_head(h, True, True)
            gdn_head(H - 1, True, False)
            gdn_tile(H - 2)
            for m in range(2):
                three(ps[:, F_BANK[m], :], m, H - 2, o_hi[:, H - 2, :], o_lo[:, H - 2, :], False, False)
            o_sum(H - 1, 2 * H)
            pe.wait_ge(s_state_done, 3 * H)
            for n in range(6 * (H - 1), 9 * (H - 1)):
                out_early(U_GDN_OUT, n, o_hi, o_lo, H - 1)

            def to_stream(base, per, r_hi, r_lo, done, tiles_done, added=s_stream_added, started=(0, 0, 0, 0)):
                nu = len(per)

                def body(i):
                    for m in range(4):
                        if due(done + i * 4 + m - 3):
                            pe.wait_ge(added, done + i * 4 + m - 3)
                        kt = 0
                        for n, count in enumerate(per):
                            u = base + (i * 4 + m) * nu + n
                            unit_ready(u)
                            for k in range(count):
                                if i == 0 and kt < started[m]:
                                    kt += 1
                                    continue
                                if i == 0 and m == 0:
                                    tiles_done(kt)
                                mm = three(ps[:, F_BANK[m], :], (m * nu + n) % 4, k, r_hi[:, kt, :], r_lo[:, kt, :],
                                           kt == 0, kt == sum(per) - 1)
                                kt += 1
                            mm.then_inc(s_unit_used, 1)
                body(0)
                body(1)

            pe.wait_ge(s_nwt_taken, H)
            to_stream(U_GDN_OUT, [8], o_hi, o_lo, 0, gdn_tile, started=(H - 1, H - 1, H - 1, 0))

            def ffn_up(layer):
                first = KT * (2, 4)[layer]

                def pair(i, q, ready):
                    for g in range(2):
                        s = 2 * q + g
                        u = U_UP[layer] + i * 4 + s
                        unit_ready(u)
                        if due(2 * FT * layer + i * 4 + s - 3):
                            pe.wait_ge(s_ffn_evacuated, 2 * FT * layer + i * 4 + s - 3)
                        for k in range(KT):
                            if ready and g == 0:
                                if due(first - KT + k + 1):
                                    pe.wait_ge(s_h_hi_done, first - KT + k + 1)
                                if due(first - KT + k + 1):
                                    pe.wait_ge(s_h_lo_done, first - KT + k + 1)
                            mm = three(ps[:, F_BANK[s], :], s, k, h_hi[:, k, :], h_lo[:, k, :], k == 0, k == KT - 1)
                        mm.then_inc(s_unit_used, 1)
                        if ready and g == 0:
                            stream_sum((2, 4)[layer])
                if due(KT * (1, 3)[layer]):
                    pe.wait_ge(s_stream_added, KT * (1, 3)[layer])
                pair(0, 0, True)
                pair(0, 1, False)
                with pe.Fori(1, 2 * FT // 4) as i:
                    pair(i, 0, False)
                    pair(i, 1, False)

            def hidden_tile(layer):
                def f(k):
                    if k >= FT - 4:
                        pe.wait_ge(s_hid_lo_done, FT * layer + k + 1)
                        pe.wait_ge(s_hid_hi_done, FT * layer + k + 1)
                return f

            def ffn_down(layer):
                pe.wait_ge(s_ffn_evacuated, 2 * FT * (layer + 1))
                if due(FT * layer + FT - 4):
                    pe.wait_ge(s_hid_lo_done, FT * layer + FT - 4)
                if due(FT * layer + FT - 4):
                    pe.wait_ge(s_hid_hi_done, FT * layer + FT - 4)
                to_stream(U_DOWN[layer], DOWN_KT, hid_hi, hid_lo, (KT, 0)[layer], hidden_tile(layer),
                          (s_stream_added, s_x_final)[layer])

            ffn_up(0)
            ffn_down(0)

            def att_project(hn, s, ready):
                for n in range(A_PASSES[s], A_PASSES[s + 1]):
                    j, k, p = n // 24, n % 24 // 3, n % 3
                    if n % 24 == 0:
                        unit_ready(U_ATT + hn * 3 + j)
                        if due(hn * 3 + j - 2):
                            pe.wait_ge(s_att_evacuated, hn * 3 + j - 2)
                    if ready and p == 0 and j == 0:
                        pe.wait_ge(s_h_hi_done, KT * 2 + k + 1)
                        pe.wait_ge(s_h_lo_done, KT * 2 + k + 1)
                    if ready and p == 0 and j == 1:
                        pe.wait_ge(s_hb_hi_done, k + 1)
                        pe.wait_ge(s_hb_lo_done, k + 1)
                    r_hi, r_lo = (hb_hi, hb_lo) if j == 1 else (h_hi, h_lo)
                    mm = three(ps[:, A_BANK[j], :], j, k, r_hi[:, k, :], r_lo[:, k, :], k == 0, k == KT - 1, (p,))
                    if n % 24 == 23:
                        mm.then_inc(s_unit_used, 1)
                if s in (11 if ready else 7, 12):
                    j = s // 12
                    if due(hn * 2 + j + 1):
                        pe.wait_ge(s_akq_squared, hn * 2 + j + 1)
                    if due(hn * 2 + j):
                        pe.wait_ge(s_akq_ms_taken, hn * 2 + j)
                    sum_partitions(B_SUM, ar[:, j, :]).then_inc(s_akq_summed, 1)

            def attend(h, s):
                if s < 3:
                    if s == 0:
                        pe.wait_ge(s_ak_normed, h + 1)
                        pe.wait_ge(s_aq_normed, h + 1)
                        if due(3 * h):
                            pe.wait_ge(s_awt_taken, 3 * h)
                    for b in ((0, 1), (2,), (3,))[s]:
                        bank, at = ((B_M, 0), (B_M, P), (B_P, 0), (B_Q, 0))[b]
                        mm = pe.matmul(ps[:, bank, at:at + P * (b + 1)], aqt[:, b * P:(b + 1) * P],
                                       akt[:, 0:P * (b + 1)], start=True, stop=True)
                    mm.then_inc(s_scores_done, 1)
                if s == 3:
                    pe.wait_ge(s_att_evacuated, 3 * h + 3)
                    if due(h):
                        pe.wait_ge(s_ao_lo_done, h)
                    each(lambda o, c: pe.transpose(o, araw[:, 2, c], aident[:]), B_O).then_inc(s_av_turned, 1)
                if s in (8, 10, 12):
                    g = (s - 8) // 2
                    if due(4 * h + (2, 3, 4)[g]):
                        pe.wait_ge(s_aw_done, 4 * h + (2, 3, 4)[g])
                    if due(6 * h + (2, 4, 6)[g]):
                        pe.wait_ge(s_sig_done, 6 * h + (2, 4, 6)[g])
                    at = 0
                    for b in ((0, 1), (2,), (3,))[g]:
                        for sb_ in range(b + 1):
                            mm = pe.transpose(ps[:, B_M + g, at:at + P], aw[:, OFF[b] + sb_ * P:OFF[b] + (sb_ + 1) * P],
                                              aident[:])
                            at += P
                    mm.then_inc(s_aw_turned, 1)
                if s in (13, 14, 15):
                    g = s - 13
                    pe.wait_ge(s_awt_taken, 3 * h + g + 1)
                    pe.wait_ge(s_av_tok_done, h + 1)
                    for b in ((0, 1), (2,), (3,))[g]:
                        for sb_ in range(b + 1):
                            mm = pe.matmul(ps[:, B_O, b * P:(b + 1) * P], avtok[:, sb_ * P:(sb_ + 1) * P],
                                           awt[:, OFF[b] + sb_ * P:OFF[b] + (sb_ + 1) * P],
                                           start=sb_ == 0, stop=sb_ == b)
                    if s == 15:
                        mm.then_inc(s_ao_done, 1)

            pe.wait_ge(s_stream_added, 2 * KT)
            for s in range(18):
                att_project(0, s, True)
                if s == 3:
                    stream_sum(3)

            def att_head(h, more):
                for s in range(18):
                    attend(h, s)
                    if more:
                        att_project(h + 1, s, False)
                    elif s < 14:
                        if s == 0:
                            pe.wait_ge(s_att_evacuated, 3 * H)
                            pe.wait_ge(s_ao_hi_done, H - 1)
                            pe.wait_ge(s_ao_lo_done, H - 1)
                        for n in range(3 * s, 3 * s + 3):
                            out_early(U_ATT_OUT, n, ao_hi, ao_lo, H - 1)

            pe.wait_ge(s_att_masks_loaded, 16 * 2)
            att_head(0, True)
            with pe.Fori(1, H - 1) as h:
                att_head(h, True)
            att_head(H - 1, False)

            def att_tile(k):
                pe.wait_ge(s_ao_lo_done, k + 1)
                pe.wait_ge(s_ao_hi_done, k + 1)

            pe.wait_ge(s_awt_taken, 3 * H)
            for n in range(6 * (H - 1), 9 * (H - 1)):
                out_early(U_ATT_OUT, n, ao_hi, ao_lo, H - 1)
            to_stream(U_ATT_OUT, [8], ao_hi, ao_lo, 2 * KT, att_tile, started=(H - 1, H - 1, H - 1, 0))
            ffn_up(1)
            ffn_down(1)

        @blk.scalar
        def _(act):
            def split_hi(u, slot, lap, cols_=8 * P, loaded=s_w_loaded, ring=AHEAD):
                act.wait_ge(loaded[slot], 16 * (lap + 1))
                if due(u - ring + 1):
                    act.wait_ge(s_unit_used, u - ring + 1)
                nc.scalar.copy(w_hi[:, slot, 0:cols_], raw[:, slot, 0:cols_]).then_inc(s_w_hi_done, 1)

            def h_hi_part(n, dst, count=s_h_hi_done, src=s_h_scaled_done):
                act.wait_ge(src, n + 1)
                nc.scalar.copy(dst, hg[:]).then_inc(count, 1)

            for k in range(KT):
                act.wait_ge(s_h_scaled_done, k + 1)
                nc.scalar.copy(h_hi[:, k, :], h_scaled[k % 2][:]).then_inc(s_h_hi_done, 1)
                if k % 2:
                    act.wait_ge(s_x_loaded[k], 16)
                    nc.scalar.activation(x_sq[k // 2][:], xs[:, k, :], ACT.Square).then_inc(s_x_squared, 1)
                if k == 1:
                    act.wait_ge(s_wab_loaded, 16)
                    nc.scalar.copy(wab_hi[:], raw[:, 3, :]).then_inc(s_wab_hi_done, 1)
                    split_hi(0, 0, 0)
            for u in range(1, AHEAD):
                split_hi(u, u, 0)

            def stream_rms(n, preload=True):
                if preload:
                    nc.scalar.preload_act_table_set(LN_EXP)
                act.wait_ge(s_stream_ms_done, n)
                nc.scalar.activation(rms[:], ms[:], ACT.Ln).then_inc(s_stream_ln, 1)
                if due(n):
                    act.wait_ge(s_stream_ln, n)
                nc.scalar.activation(rms[:], rms[:], ACT.Exp, scale=-0.5).then_inc(s_stream_guess, 1)

            stream_rms(1)
            act.wait_ge(s_params_loaded, 16)
            nc.scalar.activation(aexp[:], prm[0:H, C_ALOG:C_ALOG + 1], ACT.Exp).then_inc(s_a_exp_done, 1)
            act.wait_ge(s_neg_abs_done, 1)
            nc.scalar.activation(row2[:], row1[:], ACT.Exp).then_inc(s_e_done, 1)
            act.wait_ge(s_one_plus_e, 1)
            nc.scalar.activation(row1[:], row3[:], ACT.Ln).then_inc(s_ln_done, 1)
            act.wait_ge(s_ab_taken, 1)
            act.wait_ge(s_gb_cleared, 1)
            nc.scalar.activation(gb[32:40, :], ab[32:40, :], ACT.Sigmoid).then_inc(s_beta_done, 1)
            def decays(h):
                act.wait_ge(s_g_spread, 16 * (h + 1))
                if due(h):
                    act.wait_ge(s_q_exp_done, h)
                if due(3 * h):
                    act.wait_ge(s_cols_now, 3 * h)
                nc.scalar.activation(egb[:], gspread[:], ACT.Exp).then_inc(s_exp_g_done, 1)
                act.wait_ge(s_decay_arg, h + 1)
                nc.scalar.activation(decay[:], decay[:], ACT.Exp).then_inc(s_decay_done, 1)

            def gdn_project(hn, s, first=False):
                if s in (1, 4, 7, 10):
                    j = (1, 4, 7, 10).index(s) + 1
                    if j > 2 or not isinstance(hn, int) or hn > 0:
                        split_hi(hn * 4 + j, j % 4, hn + j // 4, ring=4)
                if s in (11, 17):
                    j = (s - 11) // 6
                    act.wait_ge(s_conv_done, 12 * hn + 4 * j + 4)
                    nc.scalar.activation(kqv[:, j, :], kqv[:, j, :], ACT.Silu).then_inc(s_kq_silu, 1)
                    act.wait_ge(s_kq_silu, 2 * hn + j + 1)
                    nc.scalar.activation(r_kq[:, j, :], kqv[:, j, :], ACT.Square).then_inc(s_kq_squared, 1)
                if s in (12, 18):
                    nc.scalar.preload_act_table_set(LN_EXP)
                if s in (14 if first else 13, 19):
                    j = s // 19
                    act.wait_ge(s_ms_taken_kq, 2 * hn + j + 1)
                    nc.scalar.activation(r_kq[:, j, :], m_kq[:, j, :], ACT.Ln).then_inc(s_kq_ln, 1)
                    act.wait_ge(s_kq_ln, 2 * hn + j + 1)
                    nc.scalar.activation(r_kq[:, j, :], r_kq[:, j, :], ACT.Exp, scale=-0.5).then_inc(s_kq_guess, 1)
                if s == (15 if first else 8):
                    decays(hn)
                if s == 23:
                    act.wait_ge(s_conv_done, 12 * hn + 12)
                    nc.scalar.activation(kqv[:, 2, :], kqv[:, 2, :], ACT.Silu).then_inc(s_v_silu, 1)

            def z_silu(h):
                act.wait_ge(s_gdn_evacuated, 4 * h + 4)
                if due(h):
                    act.wait_ge(s_o_gated, h)
                nc.scalar.activation(zs[:], zraw[:], ACT.Silu).then_inc(s_z_silu, 1)

            def o_square(h):
                act.wait_ge(s_o_taken, h + 1)
                if due(3 * h):
                    act.wait_ge(s_o_newton, 3 * h)
                nc.scalar.activation(r_kq[:, 2, :], osb[:], ACT.Square).then_inc(s_o_squared, 1)

            def o_guess(h):
                act.wait_ge(s_ms_taken_o, h + 1)
                nc.scalar.activation(r_kq[:, 2, :], m_kq[:, 2, :], ACT.Ln).then_inc(s_o_ln, 1)
                act.wait_ge(s_o_ln, h + 1)
                nc.scalar.activation(r_kq[:, 2, :], r_kq[:, 2, :], ACT.Exp, scale=-0.5).then_inc(s_o_guess, 1)

            def o_high(h):
                act.wait_ge(s_o_out, h + 1)
                nc.scalar.copy(o_hi[:, h, :], tz[:]).then_inc(s_o_hi_done, 1)

            def delta(h, s):
                if s == 0:
                    act.wait_ge(s_k_turned, h + 1)
                    if due(h):
                        act.wait_ge(s_nwt_done, h)
                    nc.scalar.copy(ktok[:], ps[:, B_T, :]).then_inc(s_k_tok_done, 1)
                if s == 1:
                    act.wait_ge(s_v_turned, h + 1)
                    if due(4 * h):
                        act.wait_ge(s_v_new_done, 4 * h)
                    nc.scalar.copy(vtok[:], ps[:, B_Q, :]).then_inc(s_v_tok_done, 1)
                if s in (3, 5, 7, 9, 11, 13):
                    k = (s - 1) // 2
                    if due(6 * h + k):
                        act.wait_ge(s_m1_done, 6 * h + k)
                    if due(6 * h + k - 1):
                        act.wait_ge(s_level_done, 6 * h + k - 1)
                    nc.scalar.copy(m1[:], ps[:, B_M, :]).then_inc(s_m1_taken, 1)
                if s == 15:
                    act.wait_ge(s_nwt_done, h + 1)
                    nc.scalar.copy(nwt[:], ps[:, B_P, :]).then_inc(s_nwt_taken, 1)
                if s in (16, 18, 20, 22):
                    c = (s - 16) // 2
                    cs = slice(c * P, (c + 1) * P)
                    act.wait_ge(s_v_new_done, 4 * h + c + 1)
                    act.wait_ge(s_cols_now, 3 * h + 3)
                    if c == 0:
                        if due(h):
                            act.wait_ge(s_o_done, h)
                    nc.scalar.activation(vn[:, cs], ps[:, B_T, cs], ACT.Copy, scale=cols[:, c:c + 1])\
                        .then_inc(s_v_scaled, 1)
                if s == 23:
                    act.wait_ge(s_o_done, h + 1)
                    if due(h):
                        act.wait_ge(s_o_gated, h)
                    nc.scalar.copy(osb[:], ps[:, B_O, :]).then_inc(s_o_taken, 1)

            for s in range(24):
                gdn_project(0, s, first=True)
                if s == 14:
                    act.wait_ge(s_g_cols_in, 2)
                    nc.scalar.activation(gcols[:, :, 4:8], gcols[:, :, 8:12], ACT.Exp).then_inc(s_exp_g_cols, 1)

            def gdn_head(h, prev, more):
                for s in range(24):
                    if more and s == 23:
                        gdn_project(h + 1, s)
                    delta(h, s)
                    if prev and s == 1:
                        o_square(h - 1)
                    if s == 4:
                        z_silu(h)
                    if more and s < 23:
                        gdn_project(h + 1, s)
                    if not more and s in (1, 4):
                        j = (1, 4).index(s) + 1
                        split_hi(U_GDN_OUT + j, j, H, ring=4)
                    if s == 6 or not more and s == 13:
                        nc.scalar.preload_act_table_set(LN_EXP)
                    if prev and s == 6:
                        o_guess(h - 1)
                    if prev and s == 12:
                        o_high(h - 1)

            gdn_head(0, False, True)
            gdn_head(1, True, True)
            with act.Fori(2, H - 1) as h:
                gdn_head(h, True, True)
            gdn_head(H - 1, True, False)
            o_square(H - 1)
            o_guess(H - 1)
            o_high(H - 1)

            def to_stream(base, per, next_gain, done, nh, last=False, ring_next=4, next_base=0):
                nu = len(per)

                def body(i):
                    for m in range(4):
                        for n in range(nu):
                            u = base + (i * 4 + m) * nu + n
                            v = (m * nu + n + AHEAD)
                            if not (last and i * 4 * nu + v >= 8 * nu):
                                over = i * 4 * nu + v - 8 * nu
                                if over >= 0 and ring_next == 3:
                                    split_hi(u + AHEAD, over, 0, loaded=s_att_w_loaded)
                                elif over >= 0:
                                    split_hi(u + AHEAD, over % 4, lap_of(u + AHEAD))
                                else:
                                    split_hi(u + AHEAD, v % 4, lap_of(u + AHEAD), per[v % nu] * P)
                        if next_gain:
                            h_hi_part(nh + i * 4 + m, h_hi[:, i * 4 + m, :])
                body(0)
                body(1)

            to_stream(U_GDN_OUT, [8], True, 0, KT)
            stream_rms(2)

            def ffn_up(layer):
                def pair(i, q, n_hid):
                    for g in range(2):
                        s = 2 * q + g
                        u = U_UP[layer] + i * 4 + s
                        split_hi(u + AHEAD, (s + AHEAD) % 4, lap_of(U_UP[layer]) + i + (s + AHEAD) // 4)
                        act.wait_ge(s_ffn_evacuated, 2 * n_hid + g + 1)
                        act.wait_ge(s_ffn_taps, (FT // 2) * layer + i + 1)
                        if due(n_hid):
                            act.wait_ge(s_hid_hi_done, n_hid)
                        if due(n_hid):
                            act.wait_ge(s_hid_lo_done, n_hid)
                        nc.scalar.activation(facc[:, g, :], fin[:, g, 0:T], ACT.Copy, scale=taps[:, 3 * s:3 * s + 1])\
                            .then_inc(s_ffn_conv_done, 1)
                        if g == 0:
                            act.wait_ge(s_ffn_conv_done, 6 * n_hid + 3)
                            nc.scalar.activation(facc[:, 0, :], facc[:, 0, :], ACT.Silu).then_inc(s_gate_silu, 1)
                    act.wait_ge(s_hidden_done, n_hid + 1)
                    nc.scalar.copy(hid_hi[:, i * 2 + q, :], fh).then_inc(s_hid_hi_done, 1)

                pair(0, 0, layer * FT)
                pair(0, 1, layer * FT + 1)
                with act.Fori(1, 2 * FT // 4) as i:
                    pair(i, 0, layer * FT + i * 2)
                    pair(i, 1, layer * FT + i * 2 + 1)

            ffn_up(0)
            to_stream(U_DOWN[0], DOWN_KT, True, KT, 2 * KT, ring_next=3)
            act.wait_ge(s_unit_used, U_ATT)
            act.dma_start(aident[:], masks[:, LEVELS * P:(LEVELS + 1) * P]).then_inc(s_att_masks_loaded, 16)
            act.dma_start(amask[:], masks[:, (LEVELS + 2) * P:(LEVELS + 3) * P]).then_inc(s_att_masks_loaded, 16)
            nc.scalar.preload_act_table_set(LN_EXP)
            for k in range(KT):
                if k == 3:
                    stream_rms(3, preload=False)
                act.wait_ge(s_hb_scaled_done, k + 1)
                nc.scalar.copy(hb_hi[:, k, :], am[:, k % 2, :]).then_inc(s_hb_hi_done, 1)

            def att_project(hn, s, last=False, first=False):
                if s in A_ENDS:
                    j = A_ENDS.index(s)
                    if last:
                        split_hi(U_ATT_OUT + j, j, lap_of(U_ATT_OUT))
                    else:
                        split_hi(U_ATT + hn * 3 + j + AHEAD, j, hn + 1, loaded=s_att_w_loaded)
                if s in (6, 11):
                    j = (6, 11).index(s)
                    if due(3 * hn + j + 1):
                        act.wait_ge(s_att_evacuated, 3 * hn + j + 1)
                    if due(hn):
                        act.wait_ge(s_aq_normed if j else s_ak_normed, hn)
                    nc.scalar.activation(ar[:, j, :], araw[:, j, :], ACT.Square).then_inc(s_akq_squared, 1)
                if s == 6:
                    nc.scalar.preload_act_table_set(LN_EXP)
                if s in (11 if first else 7, 12):
                    j = s // 12
                    if due(2 * hn + j + 1):
                        act.wait_ge(s_akq_ms_taken, 2 * hn + j + 1)
                    nc.scalar.activation(ar[:, j, :], am[:, j, :], ACT.Ln).then_inc(s_akq_ln, 1)
                    if due(2 * hn + j + 1):
                        act.wait_ge(s_akq_ln, 2 * hn + j + 1)
                    nc.scalar.activation(ar[:, j, :], ar[:, j, :], ACT.Exp, scale=-0.5).then_inc(s_akq_guess, 1)

            SCALE = float(P) ** -0.5

            def attend(h, s):
                if s < 3:
                    at, wide = ((0, 3 * P), (3 * P, 3 * P), (6 * P, 4 * P))[s]
                    if due(3 * h + s + 1):
                        act.wait_ge(s_scores_masked, 3 * h + s + 1)
                    if due(h):
                        act.wait_ge(s_ao_done, h)
                    for dst, sign in ((sfail, -SCALE), (shit, SCALE)):
                        nc.scalar.activation(dst[:, at:at + wide], ps[:, B_M + s, 0:wide], ACT.Sigmoid, scale=sign)\
                            .then_inc(s_sig_done, 1)
                if s == 3:
                    act.wait_ge(s_av_turned, h + 1)
                    if due(h):
                        act.wait_ge(s_ao_done, h)
                    nc.scalar.copy(avtok[:], ps[:, B_O, :]).then_inc(s_av_tok_done, 1)
                if s in (8, 10, 12):
                    g = (s - 8) // 2
                    at, wide = ((0, 3 * P), (3 * P, 3 * P), (6 * P, 4 * P))[g]
                    act.wait_ge(s_aw_turned, 3 * h + g + 1)
                    if due(h):
                        act.wait_ge(s_ao_done, h)
                    nc.scalar.copy(awt[:, at:at + wide], ps[:, B_M + g, 0:wide]).then_inc(s_awt_taken, 1)
                if s == 15:
                    act.wait_ge(s_ao_done, h + 1)
                    nc.scalar.copy(ao_hi[:, h, :], ps[:, B_O, :]).then_inc(s_ao_hi_done, 1)

            for s in range(18):
                att_project(0, s, first=True)

            def att_head(h, more, last=False):
                for s in range(18):
                    attend(h, s)
                    if more:
                        att_project(h + 1, s, last)

            att_head(0, True)
            with act.Fori(1, H - 2) as h:
                att_head(h, True)
            att_head(H - 2, True, True)
            att_head(H - 1, False)

            to_stream(U_ATT_OUT, [8], True, 2 * KT, 3 * KT)
            stream_rms(4)
            ffn_up(1)
            to_stream(U_DOWN[1], DOWN_KT, False, 3 * KT, 4 * KT, last=True)

        @blk.gpsimd
        def _(pool):
            nc.gpsimd.memset(ones[:], 1.0).then_inc(s_ones_set, 1)
            nc.gpsimd.memset(onesrow[:], 1.0).then_inc(s_ones_rows_set, 1)
            nc.gpsimd.memset(gb[:], 0.0).then_inc(s_gb_cleared, 1)

            def square_add(n, k, first):
                if first:
                    if due(n // KT):
                        pool.wait_ge(s_stream_summed, n // KT)
                    nc.gpsimd.tensor_tensor(sumsq[:], xs[:, k, :], xs[:, k, :], ALU.mult)\
                        .then_inc(s_sumsq_done, 1)
                else:
                    if due(n):
                        pool.wait_ge(s_sumsq_done, n)
                    nc.gpsimd.tensor_tensor(nt[:], xs[:, k, :], xs[:, k, :], ALU.mult)\
                        .then_inc(s_sq_done, 1)
                    if due(n - n_first(n)):
                        pool.wait_ge(s_sq_done, n - n_first(n))
                    nc.gpsimd.tensor_tensor(sumsq[:], sumsq[:], nt[:], ALU.add).then_inc(s_sumsq_done, 1)

            def n_first(n):
                return n // KT + KT // 2

            for k in range(KT):
                if k % 2 == 0:
                    pool.wait_ge(s_x_loaded[k], 16)
                if k == 0:
                    nc.gpsimd.tensor_tensor(sumsq[:], xs[:, k, :], xs[:, k, :], ALU.mult).then_inc(s_sumsq_done, 1)
                elif k % 2 == 0:
                    pool.wait_ge(s_sumsq_done, k)
                    nc.gpsimd.tensor_tensor(nt[:], xs[:, k, :], xs[:, k, :], ALU.mult).then_inc(s_sq_done, 1)
                    pool.wait_ge(s_sq_done, k // 2)
                    nc.gpsimd.tensor_tensor(sumsq[:], sumsq[:], nt[:], ALU.add).then_inc(s_sumsq_done, 1)
                else:
                    pool.wait_ge(s_sumsq_done, k)
                    pool.wait_ge(s_x_squared, k // 2 + 1)
                    nc.gpsimd.tensor_tensor(sumsq[:], sumsq[:], x_sq[k // 2][:], ALU.add).then_inc(s_sumsq_done, 1)

            def delta(h, s):
                if s == 1:
                    pool.wait_ge(s_c0_done, h + 1)
                    if due(4 * h):
                        pool.wait_ge(s_v_new_done, 4 * h)
                    nc.gpsimd.tensor_tensor(blocks(xt[:]), each_block(ident[:]), blocks(ct[:, 0, :]), ALU.subtract)\
                        .then_inc(s_inv_t0_done, 1)
                if 1 <= s <= 6:
                    k = s
                    if k == 3:
                        pool.wait_ge(s_c0_turned, h + 1)
                        pool.wait_ge(s_inv_t0_done, h + 1)
                    pool.wait_ge(s_lt_done, 2 * h + 2)
                    if due(6 * h + k - 3):
                        pool.wait_ge(s_m1_done, 6 * h + k - 3)
                    nc.gpsimd.tensor_tensor(blocks(ct[:, k % 3, :]), blocks(lt[:]), each_block(lvl[:, k, :]), ALU.mult)\
                        .then_inc(s_c_done, 1)

            def o_newton(h):
                r, x_ = r_kq[:, 2, :], m_kq[:, 2, :]
                pool.wait_ge(s_o_guess, h + 1)
                if due(h):
                    pool.wait_ge(s_o_out, h)
                nc.gpsimd.tensor_tensor(n_o[:], r, r, ALU.mult).then_inc(s_o_newton, 1)
                pool.wait_ge(s_o_newton, 3 * h + 1)
                nc.gpsimd.tensor_tensor(n_o[:], n_o[:], x_, ALU.mult).then_inc(s_o_newton, 1)
                pool.wait_ge(s_o_gated, h + 1)
                nc.gpsimd.tensor_tensor(tz[:], tz[:], r, ALU.mult).then_inc(s_o_newton, 1)

            pool.wait_ge(s_masks_loaded, 16 * 3)

            def gdn_head(h, prev):
                for s in range(7):
                    delta(h, s)
                if prev:
                    o_newton(h - 1)

            gdn_head(0, False)
            gdn_head(1, True)
            with pool.Fori(2, H) as h:
                gdn_head(h, True)

            def to_stream(n):
                for k in range(KT):
                    if due(n - KT + k + 1):
                        pool.wait_ge(s_stream_added, n - KT + k + 1)
                    square_add(n + k, k, k == 0)

            to_stream(KT)
            to_stream(2 * KT)
            for b in range(NB):
                at = OFF[b] + b + P * (b + 1)
                nc.gpsimd.memset(surv[:, at:at + 1], 1.0).then_inc(s_aones_set, 1)
            to_stream(3 * KT)

        @blk.vector
        def _(dve):
            def split_lo(u, slot, cols_=8 * P):
                dve.wait_ge(s_w_hi_done, u + 1)
                nc.vector.tensor_tensor(w_lo[:, slot, 0:cols_], raw[:, slot, 0:cols_],
                                        w_hi[:, slot, 0:cols_].bitcast(F32), ALU.subtract)\
                    .then_inc(s_w_lo_done, 1)

            def h_scale(n, k, gain, count=s_h_scaled_done, lo_count=s_h_lo_done):
                if due(n):
                    dve.wait_ge(lo_count, n)
                nc.vector.tensor_scalar(hg[:], xs[:, k, :], gain, None, ALU.mult).then_inc(count, 1)

            def h_low(n, k, hi, lo, hi_count=s_h_hi_done, lo_count=s_h_lo_done):
                dve.wait_ge(hi_count, n + 1)
                nc.vector.tensor_tensor(lo[:, k, :], hg[:], hi[:, k, :].bitcast(F32), ALU.subtract)\
                    .then_inc(lo_count, 1)

            def newton(count, n, t, r, x_, dst, dst_count):
                newton_start(count, n, t, r, x_)
                newton_end(count, n, t, r, dst, dst_count)

            def newton_start(count, n, t, r, x_):
                nc.vector.tensor_tensor(t, r, r, ALU.mult).then_inc(count, 1)
                dve.wait_ge(count, 3 * n + 1)
                nc.vector.tensor_tensor(t, t, x_, ALU.mult).then_inc(count, 1)

            def newton_end(count, n, t, r, dst, dst_count):
                dve.wait_ge(count, 3 * n + 2)
                nc.vector.tensor_scalar(t, t, -0.5, 1.5, ALU.mult, ALU.add).then_inc(count, 1)
                dve.wait_ge(count, 3 * n + 3)
                nc.vector.tensor_tensor(dst, r, t, ALU.mult).then_inc(dst_count, 1)

            def stream_ms(n):
                dve.wait_ge(s_stream_summed, n)
                nc.vector.tensor_scalar(ms[:], ps[:, B_SUM, :], 1.0 / D, EPS, ALU.mult, ALU.add)\
                    .then_inc(s_stream_ms_done, 1)

            def stream_newton(n):
                dve.wait_ge(s_stream_guess, n)
                newton(s_rms_newton, n - 1, hg[:], rms[:], ms[:], rms[:], s_rms_done)

            def stream_rms(n):
                stream_ms(n)
                stream_newton(n)

            dve.wait_ge(s_params_loaded, 16)
            def two_tiles_split(k, scale_gain, buf, scaled, hi, hi_done, lo, lo_done):
                if k < KT:
                    if k > 1:
                        dve.wait_ge(lo_done, k - 1)
                    g0 = scale_gain + k
                    nc.vector.tensor_scalar(buf[k % 2], xs[:, k, :], prm[:, g0:g0 + 1], None, ALU.mult)\
                        .then_inc(scaled, 1)
                if k > 0:
                    dve.wait_ge(hi_done, k)
                    nc.vector.tensor_tensor(lo[:, k - 1, :], buf[(k - 1) % 2], hi[:, k - 1, :].bitcast(F32),
                                            ALU.subtract).then_inc(lo_done, 1)

            for k in range(KT + 1):
                if k < KT:
                    dve.wait_ge(s_x_loaded[k], 16)
                two_tiles_split(k, G_NORM["a"], [b[:] for b in h_scaled], s_h_scaled_done, h_hi, s_h_hi_done,
                                h_lo, s_h_lo_done)
                if k == 2:
                    dve.wait_ge(s_wab_hi_done, 1)
                    nc.vector.tensor_tensor(wab_lo[:], raw[:, 3, :], wab_hi[:].bitcast(F32), ALU.subtract)\
                        .then_inc(s_wab_split, 2)
                    split_lo(0, 0)
            for u in range(1, AHEAD):
                split_lo(u, u)
            nc.vector.memset(cin[:, 0:3], 0.0).then_inc(s_conv_pads, 1)
            stream_rms(1)

            def conv_tap(hn, jj, tap):
                src, w = cin[:, tap:tap + T], taps[:, 4 * jj + tap:4 * jj + tap + 1]
                if due(4 * hn + jj + 1):
                    dve.wait_ge(s_gdn_evacuated, 4 * hn + jj + 1)
                dve.wait_ge(s_taps_now, hn + 1)
                if tap == 0:
                    dve.wait_ge(s_conv_pads, 1)
                    if due(hn):
                        dve.wait_ge(s_kq_done, hn)
                    if due(hn):
                        dve.wait_ge(s_q_exp_done, hn)
                    if due(hn):
                        dve.wait_ge(s_v_turned, hn)
                    nc.vector.tensor_scalar(kqv[:, jj, :], src, w, None, ALU.mult).then_inc(s_conv_done, 1)
                else:
                    if due(12 * hn + 4 * jj + tap):
                        dve.wait_ge(s_conv_done, 12 * hn + 4 * jj + tap)
                    nc.vector.scalar_tensor_tensor(kqv[:, jj, :], src, w, kqv[:, jj, :], ALU.mult, ALU.add)\
                        .then_inc(s_conv_done, 1)

            nc.vector.tensor_copy(taps[:], prm[:, C_GDN_CONV:C_GDN_CONV + 12]).then_inc(s_taps_now, 1)
            dve.wait_ge(s_unit_used, 1)
            dve.wait_ge(s_rms_done, 1)
            nc.vector.tensor_tensor(cin[:, 3:], ps[:, 0, :], rms[:], ALU.mult).then_inc(s_gdn_evacuated, 1)
            dve.wait_ge(s_ab_summed, 1)
            nc.vector.tensor_tensor(ab[:], ps[0:40, B_M, :], rms[0:40, :], ALU.mult).then_inc(s_ab_taken, 1)
            dve.wait_ge(s_ab_taken, 1)
            nc.vector.tensor_scalar(row3[:], ab[0:H, :], prm[0:H, C_DT:C_DT + 1], None, ALU.add)\
                .then_inc(s_row_step, 1)
            dve.wait_ge(s_row_step, 1)
            nc.vector.scalar_tensor_tensor(row1[:], row3[:], -1.0, row3[:], ALU.mult, ALU.min)\
                .then_inc(s_neg_abs_done, 1)
            dve.wait_ge(s_gb_cleared, 1)
            nc.vector.tensor_scalar(ab[0:H, :], row3[:], 0.0, None, ALU.max).then_inc(s_row_step, 1)
            conv_tap(0, 0, 0)
            conv_tap(0, 0, 1)
            dve.wait_ge(s_e_done, 1)
            dve.wait_ge(s_row_step, 2)
            nc.vector.tensor_scalar(row3[:], row2[:], 1.0, None, ALU.add).then_inc(s_one_plus_e, 1)
            conv_tap(0, 0, 2)
            conv_tap(0, 0, 3)
            dve.wait_ge(s_ln_done, 1)
            nc.vector.scalar_tensor_tensor(row3[:], row3[:], 1.0, row2[:], ALU.subtract, ALU.subtract)\
                .then_inc(s_row_step, 1)
            dve.wait_ge(s_row_step, 3)
            nc.vector.tensor_tensor(row1[:], row1[:], row3[:], ALU.subtract).then_inc(s_row_step, 1)
            dve.wait_ge(s_row_step, 4)
            nc.vector.tensor_tensor(row1[:], row1[:], ab[0:H, :], ALU.add).then_inc(s_row_step, 1)
            dve.wait_ge(s_row_step, 5)
            dve.wait_ge(s_a_exp_done, 1)
            nc.vector.tensor_scalar(row1[:], row1[:], aexp[:], -1.0, ALU.mult, ALU.mult).then_inc(s_row_step, 1)
            dve.wait_ge(s_row_step, 6)
            dve.wait_ge(s_ones_rows_set, 1)
            for c in range(NB):
                cs = slice(c * P, (c + 1) * P)
                ins = nc.vector.tensor_tensor_scan(gb[0:H, cs], onesrow[:, cs], row1[:, cs], 0.0, ALU.mult, ALU.add)
                ins.then_inc(s_g_scanned, 1)

            def gdn_project(hn, s, first=False):
                j = s // 6
                if s == 0:
                    if due(12 * hn):
                        dve.wait_ge(s_conv_done, 12 * hn)
                    nc.vector.tensor_copy(taps[:], prm[:, C_GDN_CONV:C_GDN_CONV + 12 * H]
                                          .rearrange("p (h t) -> p h t", h=H)[:, hn, :]).then_inc(s_taps_now, 1)
                if s % 6 == 5:
                    u = hn * 4 + j
                    dve.wait_ge(s_unit_used, u + 1)
                    if j < 3:
                        if due(12 * hn + 4 * j):
                            dve.wait_ge(s_conv_done, 12 * hn + 4 * j)
                        dst = cin[:, 3:]
                    else:
                        if due(hn):
                            dve.wait_ge(s_z_silu, hn)
                        dst = zraw[:]
                    nc.vector.tensor_tensor(dst, ps[:, j % 2, :], rms[:], ALU.mult).then_inc(s_gdn_evacuated, 1)
                if s in (4, 7, 9, 11):
                    v = (4, 7, 9, 11).index(s) + 1
                    if v > 2 or not isinstance(hn, int) or hn > 0:
                        split_lo(hn * 4 + v, v % 4)
                if s == (15 if first else 6):
                    dve.wait_ge(s_g_spread, 16 * (hn + 1))
                    dve.wait_ge(s_g_cols_in, 1)
                    nc.vector.tensor_tensor(blocks(decay[:]), blocks(gspread[:]), per_block(gcols[:, hn, 8:12]),
                                            ALU.subtract).then_inc(s_g_diff, 1)
                    dve.wait_ge(s_g_diff, hn + 1)
                    nc.vector.tensor_tensor(blocks(decay[:]), blocks(decay[:]), each_block(tri[:]), ALU.min)\
                        .then_inc(s_decay_arg, 1)
                if 7 <= s <= 22 and 1 <= s % 6 <= 4 and not (first and s < 12):
                    conv_tap(hn, s // 6 - 1, s % 6 - 1)
                if s in (14 if first else 12, 18):
                    q = s // 18
                    if due(2 * hn + q + 1):
                        dve.wait_ge(s_kq_summed, 2 * hn + q + 1)
                    if due(3 * (2 * hn + q) - 3):
                        dve.wait_ge(s_kn_steps, 3 * (2 * hn + q) - 3)
                    nc.vector.tensor_scalar(m_kq[:, q, :], ps[:, B_SUM, :], EPS, None, ALU.add)\
                        .then_inc(s_ms_taken_kq, 1)
                if s in (15, 20):
                    q = (s - 15) // 5
                    dve.wait_ge(s_kq_guess, 2 * hn + q + 1)
                    newton_start(s_kn_steps, 2 * hn + q, n_k[:], r_kq[:, q, :], m_kq[:, q, :])
                if s in (17, 21):
                    q = (s - 17) // 4
                    newton_end(s_kn_steps, 2 * hn + q, n_k[:], r_kq[:, q, :], r_kq[:, q, :], s_kq_rnorm)
                    dve.wait_ge(s_kq_rnorm, 2 * hn + q + 1)
                    if q == 0:
                        nc.vector.tensor_tensor(kn, kn, r_kq[:, 0, :], ALU.mult).then_inc(s_k_normed, 1)
                    else:
                        nc.vector.scalar_tensor_tensor(qn, qn, float(P) ** -0.5, r_kq[:, 1, :],
                                                       ALU.mult, ALU.mult).then_inc(s_q_normed, 1)

            def o_gate(h):
                dve.wait_ge(s_o_taken, h + 1)
                dve.wait_ge(s_z_silu, h + 1)
                if due(h):
                    dve.wait_ge(s_o_hi_done, h)
                if due(h):
                    dve.wait_ge(s_o_lo_done, h)
                nc.vector.scalar_tensor_tensor(tz[:], osb[:], prm[:, C_OGAIN:C_OGAIN + 1], zs[:], ALU.mult, ALU.mult)\
                    .then_inc(s_o_gated, 1)

            def o_mean(h):
                dve.wait_ge(s_o_summed, h + 1)
                if due(3 * h):
                    dve.wait_ge(s_o_newton, 3 * h)
                nc.vector.tensor_scalar(m_kq[:, 2, :], ps[:, B_SUM, :], 1.0 / P, EPS, ALU.mult, ALU.add)\
                    .then_inc(s_ms_taken_o, 1)

            def o_scale(h):
                dve.wait_ge(s_o_newton, 3 * h + 3)
                nc.vector.tensor_scalar(n_o[:], n_o[:], -0.5, 1.5, ALU.mult, ALU.add).then_inc(s_o_correction, 1)
                dve.wait_ge(s_o_correction, h + 1)
                nc.vector.tensor_tensor(tz[:], tz[:], n_o[:], ALU.mult).then_inc(s_o_out, 1)

            def o_low(h):
                dve.wait_ge(s_o_hi_done, h + 1)
                nc.vector.tensor_tensor(o_lo[:, h, :], tz[:], o_hi[:, h, :].bitcast(F32), ALU.subtract)\
                    .then_inc(s_o_lo_done, 1)

            def delta(h, s):
                if s == 0:
                    if due(4 * h):
                        dve.wait_ge(s_v_scaled, 4 * h)
                    if due(3 * h):
                        dve.wait_ge(s_state_done, 3 * h)
                    dve.wait_ge(s_g_cols_done, 1)
                    dve.wait_ge(s_decay_done, h + 1)
                    ends = slice(P - 1, T, P)
                    nc.vector.tensor_copy(cols[:, 0:8], gcols[:, h, 0:8]).then_inc(s_cols_now, 1)
                    nc.vector.tensor_copy(cols[:, 8:12], egb[:, ends]).then_inc(s_cols_now, 1)
                    nc.vector.tensor_copy(cols[:, 12:16], decay[:, ends]).then_inc(s_cols_now, 1)
                    dve.wait_ge(s_kk_done, h + 1)
                    if due(6 * h):
                        dve.wait_ge(s_c_done, 6 * h)
                    nc.vector.tensor_tensor(lt[:], ps[:, B_M, :], decay[:], ALU.mult).then_inc(s_lt_done, 1)
                    dve.wait_ge(s_lt_done, 2 * h + 1)
                    dve.wait_ge(s_cols_now, 3 * h + 3)
                    nc.vector.tensor_tensor(blocks(lt[:]), blocks(lt[:]), per_block(cols[:, 0:4]), ALU.mult)\
                        .then_inc(s_lt_done, 1)
                    dve.wait_ge(s_lt_done, 2 * h + 2)
                    if due(6 * h):
                        dve.wait_ge(s_m1_done, 6 * h)
                    nc.vector.tensor_tensor(blocks(ct[:, 0, :]), blocks(lt[:]), each_block(lvl[:, 0, :]), ALU.mult)\
                        .then_inc(s_c0_done, 1)
                    dve.wait_ge(s_k_turned, h + 1)
                    dve.wait_ge(s_k_tok_done, h + 1)
                    if due(3 * h):
                        dve.wait_ge(s_state_summed, 3 * h)
                    nc.vector.tensor_tensor(blocks(kdec[:]), blocks(ps[:, B_T, :]), per_block(cols[:, 12:16]), ALU.mult)\
                        .then_inc(s_k_dec_done, 1)
                if s == 2:
                    dve.wait_ge(s_c0_turned, h + 1)
                    nc.vector.tensor_tensor(blocks(xm[:]), each_block(ident[:]), blocks(ps[:, B_M, :]), ALU.subtract)\
                        .then_inc(s_inv_done, 1)
                    dve.wait_ge(s_kq_done, h + 1)
                    if due(h):
                        dve.wait_ge(s_o_done, h)
                    nc.vector.tensor_tensor(qkt[:], ps[:, B_P, :], decay[:], ALU.mult).then_inc(s_qkt_done, 1)
                    dve.wait_ge(s_q_normed, h + 1)
                    nc.vector.tensor_tensor(qe[:], qn, egb[:], ALU.mult).then_inc(s_q_exp_done, 1)
                if s in (4, 6, 8, 10, 12, 14):
                    k = (s - 2) // 2
                    if due(6 * h + k):
                        dve.wait_ge(s_level_done, 6 * h + k)
                    if k < 6:
                        if due(6 * h + k):
                            dve.wait_ge(s_inv_done, 6 * h + k)
                        nc.vector.tensor_tensor(half(xm[:], k, 0), half(xm[:], k, 0),
                                                whole(ps[:, B_P, 0:T // 2], k), ALU.subtract).then_inc(s_inv_done, 1)
                    if due(6 * h + k - 1):
                        dve.wait_ge(s_inv_t_done, 6 * h + k - 1)
                    dve.wait_ge(s_inv_t0_done, h + 1)
                    nc.vector.tensor_tensor(half(xt[:], k, 1), half(xt[:], k, 1),
                                            whole(ps[:, B_Q, 0:T // 2], k), ALU.subtract).then_inc(s_inv_t_done, 1)
                if s == 14:
                    dve.wait_ge(s_inv_t_done, 6 * h + 6)
                    nc.vector.tensor_tensor(blocks(xte[:]), blocks(xt[:]), per_block(cols[:, 4:8]), ALU.mult)\
                        .then_inc(s_inv_te_done, 1)
                if s in (17, 19, 21):
                    c = (s - 17) // 2
                    dve.wait_ge(s_state_summed, 3 * h + c + 1)
                    if c == 0:
                        if due(h):
                            dve.wait_ge(s_o_done, h)
                        nc.vector.tensor_copy(st[:], ps[:, B_M, 0:P]).then_inc(s_state_done, 1)
                    else:
                        if due(3 * h + c):
                            dve.wait_ge(s_state_done, 3 * h + c)
                        nc.vector.scalar_tensor_tensor(st[:], st[:], cols[:, 8 + c:9 + c], ps[:, B_M, 0:P],
                                                       ALU.mult, ALU.add).then_inc(s_state_done, 1)

            for s in range(6, 24):
                if s == 15:
                    dve.wait_ge(s_gb_turned, 1)
                    turned = ps[:, B_T, 0:NB * 40].rearrange("p (c r) -> p r c", c=NB)
                    nc.vector.tensor_copy(gcols[:, :, 8:12], turned[:, 0:H, :]).then_inc(s_g_cols_in, 1)
                    nc.vector.tensor_copy(gcols[:, :, 0:4], turned[:, 32:40, :]).then_inc(s_g_cols_in, 1)
                gdn_project(0, s, first=True)
                if s == 17:
                    dve.wait_ge(s_exp_g_cols, 1)
                    nc.vector.tensor_scalar(gcols[:, :, 4:8], gcols[:, :, 4:8], -1.0, None, ALU.mult)\
                        .then_inc(s_g_cols_done, 1)

            def gdn_head(h, prev, more):
                for s in range(24):
                    delta(h, s)
                    if prev and s == 3:
                        o_mean(h - 1)
                        o_gate(h - 1)
                    if prev and s == 10:
                        o_scale(h - 1)
                    if more:
                        gdn_project(h + 1, s)
                    if not more and s in (4, 7):
                        split_lo(U_GDN_OUT + (4, 7).index(s) + 1, (4, 7).index(s) + 1)
                    if prev and s == 14:
                        o_low(h - 1)

            gdn_head(0, False, True)
            gdn_head(1, True, True)
            with dve.Fori(2, H - 1) as h:
                gdn_head(h, True, True)
            gdn_head(H - 1, True, False)
            o_gate(H - 1)
            o_mean(H - 1)
            dve.wait_ge(s_o_guess, H)
            newton_start(s_o_newton, H - 1, n_o[:], r_kq[:, 2, :], m_kq[:, 2, :])
            dve.wait_ge(s_o_gated, H)
            nc.vector.tensor_tensor(tz[:], tz[:], r_kq[:, 2, :], ALU.mult).then_inc(s_o_newton, 1)
            o_scale(H - 1)
            o_low(H - 1)

            def to_stream(base, per, gain, done, nh, last=False, ring_next=4):
                nu = len(per)

                def body(i):
                    for m in range(4):
                        k = i * 4 + m
                        for n in range(nu):
                            u = base + k * nu + n
                            v = m * nu + n + AHEAD
                            dve.wait_ge(s_unit_used, u + 1)
                            if n == nu - 1:
                                ins = nc.vector.tensor_tensor(xs[:, k, :], xs[:, k, :], ps[:, F_BANK[m], :], ALU.add)
                                ins.then_inc(s_x_final if last else s_stream_added, 1)
                            if not (last and i * 4 * nu + v >= 8 * nu):
                                if i * 4 * nu + v >= 8 * nu:
                                    split_lo(u + AHEAD, (i * 4 * nu + v - 8 * nu) % ring_next)
                                else:
                                    split_lo(u + AHEAD, v % 4, per[v % nu] * P)
                        if gain:
                            dve.wait_ge(s_stream_added, done + k + 1)
                            g0 = G_NORM[gain] + k
                            h_scale(nh + k, k, prm[:, g0:g0 + 1])
                            h_low(nh + k, k, h_hi, h_lo)
                body(0)
                body(1)

            to_stream(U_GDN_OUT, [8], "ffn0", 0, KT)
            stream_rms(2)

            def ffn_up(layer):
                def taps_for(i):
                    n_pair = layer * FT + i * 2
                    if due(6 * n_pair):
                        dve.wait_ge(s_ffn_conv_done, 6 * n_pair)
                    nc.vector.tensor_copy(taps[:], prm[:, C_FFN_CONV + 6 * FT * layer:C_FFN_CONV + 6 * FT * (layer + 1)]
                                          .rearrange("p (i t) -> p i t", i=FT // 2)[:, i, :])\
                        .then_inc(s_ffn_taps, 1)

                def pair(i, q):
                    n = layer * FT + i * 2 + q
                    for g in range(2):
                        s = 2 * q + g
                        u = U_UP[layer] + i * 4 + s
                        dve.wait_ge(s_unit_used, u + 1)
                        if due(6 * n):
                            dve.wait_ge(s_ffn_conv_done, 6 * n)
                        nc.vector.tensor_tensor(fin[:, g, 2:], ps[:, F_BANK[s], :], rms[:], ALU.mult)\
                            .then_inc(s_ffn_evacuated, 1)
                        split_lo(u + AHEAD, (s + AHEAD) % 4)
                        dve.wait_ge(s_ffn_evacuated, 2 * n + g + 1)
                        for tap in (1, 2):
                            dve.wait_ge(s_ffn_conv_done, 6 * n + 3 * g + tap)
                            nc.vector.scalar_tensor_tensor(facc[:, g, :], fin[:, g, tap:tap + T],
                                                           taps[:, 3 * s + tap:3 * s + tap + 1], facc[:, g, :],
                                                           ALU.mult, ALU.add).then_inc(s_ffn_conv_done, 1)
                    dve.wait_ge(s_gate_silu, n + 1)
                    dve.wait_ge(s_ffn_conv_done, 6 * n + 6)
                    if due(n):
                        dve.wait_ge(s_hid_hi_done, n)
                    if due(n):
                        dve.wait_ge(s_hid_lo_done, n)
                    nc.vector.tensor_tensor(fh, facc[:, 0, :], facc[:, 1, :], ALU.mult).then_inc(s_hidden_done, 1)
                    dve.wait_ge(s_hid_hi_done, n + 1)
                    nc.vector.tensor_tensor(hid_lo[:, i * 2 + q, :], fh, hid_hi[:, i * 2 + q, :].bitcast(F32),
                                            ALU.subtract).then_inc(s_hid_lo_done, 1)

                if layer == 0:
                    nc.vector.memset(fin[:, :, 0:2], 0.0).then_inc(s_ffn_pads, 1)
                    dve.wait_ge(s_ffn_pads, 1)
                else:
                    nc.vector.memset(fin[:, :, 0:2], 0.0).then_inc(s_ffn_pads, 1)
                    dve.wait_ge(s_ffn_pads, 2)
                if due(2 + 2 * layer):
                    dve.wait_ge(s_rms_done, 2 + 2 * layer)
                taps_for(0)
                pair(0, 0)
                pair(0, 1)
                with dve.Fori(1, FT // 2) as i:
                    taps_for(i)
                    pair(i, 0)
                    pair(i, 1)

            ffn_up(0)
            to_stream(U_DOWN[0], DOWN_KT, "kv", KT, 2 * KT, ring_next=3)
            dve.wait_ge(s_unit_used, U_ATT)
            for k in range(KT + 1):
                if k == 3:
                    stream_ms(3)
                if k == 5:
                    stream_newton(3)
                two_tiles_split(k, G_NORM["b"], [am[:, b, :] for b in range(2)], s_hb_scaled_done, hb_hi,
                                s_hb_hi_done, hb_lo, s_hb_lo_done)

            def att_project(hn, s, first=False):
                if s in A_ENDS:
                    j = A_ENDS.index(s)
                    u = U_ATT + hn * 3 + j
                    dve.wait_ge(s_unit_used, u + 1)
                    if j < 2:
                        if due(3 * hn):
                            dve.wait_ge(s_scores_done, 3 * hn)
                    else:
                        if due(hn):
                            dve.wait_ge(s_av_turned, hn)
                    nc.vector.tensor_tensor(araw[:, j, :], ps[:, A_BANK[j], :], rms[:], ALU.mult)\
                        .then_inc(s_att_evacuated, 1)
                    split_lo(u + AHEAD, j)
                if s in (11 if first else 7, 12):
                    q = s // 12
                    if due(2 * hn + q + 1):
                        dve.wait_ge(s_akq_summed, 2 * hn + q + 1)
                    nc.vector.tensor_scalar(am[:, q, :], ps[:, B_SUM, :], 1.0 / P, EPS, ALU.mult, ALU.add)\
                        .then_inc(s_akq_ms_taken, 1)
                if s in (12 if first else 8, 13):
                    q = s // 13
                    dve.wait_ge(s_akq_guess, 2 * hn + q + 1)
                    newton_start(s_akq_newton, 2 * hn + q, hg[:], ar[:, q, :], am[:, q, :])
                if s in (12, 13):
                    q = s // 13
                    newton_end(s_akq_newton, 2 * hn + q, hg[:], ar[:, q, :], ar[:, q, :], s_akq_rnorm)
                    dve.wait_ge(s_akq_rnorm, 2 * hn + q + 1)
                    c = (C_KGAIN, C_QGAIN)[q]
                    nc.vector.scalar_tensor_tensor(araw[:, q, :], araw[:, q, :], prm[:, c:c + 1], ar[:, q, :],
                                                   ALU.mult, ALU.mult).then_inc((s_ak_normed, s_aq_normed)[q], 1)

            def attend(h, s):
                if s < 3:
                    if due(3 * h + s + 1):
                        dve.wait_ge(s_scores_done, 3 * h + s + 1)
                    diag = ((B_M, 0), (B_M, 2 * P)), ((B_P, 2 * P),), ((B_Q, 3 * P),)
                    for bank, at in diag[s]:
                        ins = nc.vector.tensor_tensor(ps[:, bank, at:at + P], ps[:, bank, at:at + P], amask[:], ALU.add)
                    ins.then_inc(s_scores_masked, 1)
                if 3 <= s <= 6:
                    b = s - 3
                    n, at = P * (b + 1), OFF[b] + b
                    if due(6 * h + (2, 2, 4, 6)[b]):
                        dve.wait_ge(s_sig_done, 6 * h + (2, 2, 4, 6)[b])
                    dve.wait_ge(s_aones_set, NB)
                    f = sfail[:, OFF[b]:OFF[b] + n]
                    e = surv[:, at:at + n]
                    nc.vector.tensor_tensor_scan(e[:, ::-1], f[:, ::-1], ones[:, 0:1].to_broadcast([P, n]), 1.0, ALU.mult, ALU.mult)\
                        .then_inc(s_scan_done, 1)
                    if due(4 * h + b + 1):
                        dve.wait_ge(s_scan_done, 4 * h + b + 1)
                    nc.vector.tensor_tensor(aw[:, OFF[b]:OFF[b] + n], shit[:, OFF[b]:OFF[b] + n],
                                            surv[:, at + 1:at + 1 + n], ALU.mult).then_inc(s_aw_done, 1)
                if s == 15:
                    dve.wait_ge(s_ao_hi_done, h + 1)
                    nc.vector.tensor_tensor(ao_lo[:, h, :], ps[:, B_O, :], ao_hi[:, h, :].bitcast(F32), ALU.subtract)\
                        .then_inc(s_ao_lo_done, 1)

            dve.wait_ge(s_rms_done, 3)
            for s in range(18):
                att_project(0, s, first=True)
            dve.wait_ge(s_att_masks_loaded, 32)

            def att_head(h, more):
                for s in range(18):
                    attend(h, s)
                    if more:
                        att_project(h + 1, s)

            att_head(0, True)
            with dve.Fori(1, H - 1) as h:
                att_head(h, True)
            att_head(H - 1, False)

            to_stream(U_ATT_OUT, [8], "ffn1", 2 * KT, 3 * KT)
            stream_rms(4)
            ffn_up(1)
            to_stream(U_DOWN[1], DOWN_KT, None, 3 * KT, 4 * KT, last=True)


def tiles(w, order):
    k, m = w.shape
    t = w.reshape(k // P, P, m // P, P).transpose(2, 1, 0, 3).reshape(m // P, P, k)
    return t[order]


def constants():
    j, i = np.arange(P)[:, None], np.arange(P)[None, :]
    m = np.zeros((P, (LEVELS + 3) * P), np.float32)
    for k in range(LEVELS):
        m[:, k * P:(k + 1) * P] = ((j >> k) % 2 == 0) & ((i >> k) % 2 == 1) & (j >> (k + 1) == i >> (k + 1))
    m[:, LEVELS * P:(LEVELS + 1) * P] = i == j
    m[:, (LEVELS + 1) * P:(LEVELS + 2) * P] = np.where(i >= j, 0.0, NEG)
    m[:, (LEVELS + 2) * P:(LEVELS + 3) * P] = np.where(i >= j, NEG, 0.0)
    return m


def kernel(x, a_norm, a_w_in, a_conv, a_log, a_dt_bias, a_out_norm, a_w_out, kv_norm, w_kv, k_norm,
           b_norm, b_w_q, q_norm, b_w_out, ffn_norm, ffn_w_up, ffn_conv, ffn_w_down):
    import concourse.bacc as bacc
    from concourse.bass_utils import run_bass_kernel_spmd

    arr = np.asarray
    x, w_in = arr(x), arr(a_w_in)[0]
    units = np.zeros((UNITS, P, 8 * P), np.float32)
    units[U_GDN:U_GDN_OUT] = tiles(w_in[:, :4 * D], [t for h in range(H) for t in (H + h, h, 2 * H + h, 3 * H + h)])
    units[U_GDN_OUT:U_UP[0]] = tiles(arr(a_w_out)[0], range(KT))
    for l in range(2):
        units[U_UP[l]:U_DOWN[l]] = tiles(arr(ffn_w_up)[l], [t for f in range(FT) for t in (f, FT + f)])
        down = tiles(arr(ffn_w_down)[l], range(KT))
        for n in range(3):
            wide = DOWN_KT[n] * P
            units[U_DOWN[l] + n:U_DOWN[l] + 3 * KT:3, :, :wide] = down[:, :, 8 * P * n:8 * P * n + wide]
    kv = tiles(arr(w_kv), range(2 * H))
    units[U_ATT:U_ATT_OUT:3] = kv[:H]
    units[U_ATT + 1:U_ATT_OUT:3] = tiles(arr(b_w_q)[0], range(H))
    units[U_ATT + 2:U_ATT_OUT:3] = kv[H:]
    units[U_ATT_OUT:U_UP[1]] = tiles(arr(b_w_out)[0], range(KT))
    ab = np.zeros((D, P), np.float32)
    ab[:, 0:H] = w_in[:, 4 * D:4 * D + H]
    ab[:, 32:32 + H] = w_in[:, 4 * D + H:]
    prm = np.zeros((P, PARAMS), np.float32)
    for name, g in (("a", arr(a_norm)[0]), ("ffn0", arr(ffn_norm)[0]), ("kv", arr(kv_norm)),
                    ("b", arr(b_norm)[0]), ("ffn1", arr(ffn_norm)[1])):
        prm[:, G_NORM[name]:G_NORM[name] + KT] = g.reshape(KT, P).T
    conv = arr(a_conv)[0].reshape(4, 3, H, P)[:, [1, 0, 2]]
    prm[:, C_GDN_CONV:C_FFN_CONV] = conv.transpose(3, 2, 1, 0).reshape(P, -1)
    fconv = arr(ffn_conv).reshape(2, 3, 2, FT, P)
    prm[:, C_FFN_CONV:C_OGAIN] = fconv.transpose(4, 0, 3, 2, 1).reshape(P, -1)
    prm[:, C_OGAIN], prm[:, C_KGAIN], prm[:, C_QGAIN] = arr(a_out_norm)[0], arr(k_norm), arr(q_norm)[0]
    prm[0:H, C_ALOG], prm[0:H, C_DT] = arr(a_log)[0], arr(a_dt_bias)[0]
    ins = {
        "x": np.ascontiguousarray(x[0].T.reshape(KT, P, T)),
        "weights": units,
        "w_ab": np.ascontiguousarray(tiles(ab, [0])[0]),
        "params": prm,
        "masks": constants(),
    }
    nc = bacc.Bacc("TRN2", target_bir_lowering=False, num_devices=1)
    args = [nc.dram_tensor(f"in_{n}", a.shape, F32, kind="ExternalInput").ap() for n, a in ins.items()]
    out = nc.dram_tensor("out_t", (KT, P, T), F32, kind="ExternalOutput").ap()
    g_rows = nc.dram_tensor("g_rows", (H, T), F32, kind="Internal").ap()
    trunk(nc, *args, out, g_rows)
    r = run_bass_kernel_spmd(nc, [{f"in_{n}": a for n, a in ins.items()}], core_ids=[0])
    got = r.results[0]["out_t"]
    return np.ascontiguousarray(np.asarray(got).reshape(D, T).T).reshape(1, T, D)
```
